# Optimizing a Trainium2 kernel written in Bass

```python
import math
import jax, jax.numpy as jnp
from jax import lax
import numpy as np

D_MODEL = 1024
BATCH = 1
SEQ = 512
DEPTH = 1

GRID_W = 64
D_MIX = D_MODEL
EPS = 1e-6
CONV_W = 256
CONV_K = 3
NA_HEADS = 4
NA_DH = 64
NA_W = NA_HEADS * NA_DH
NA_KH = 8
NA_KW = 16
GDN_HEADS = 4
GDN_DK = 128
GDN_DV = 128
GDN_W = GDN_HEADS * GDN_DV
GDN_CONV_K = 3
GDN_CHUNK = 64
GDN_QKV = 2 * GDN_HEADS * GDN_DK + GDN_W
IN_SPLITS = (CONV_W, CONV_W, CONV_W, NA_W, NA_W, NA_W, GDN_QKV, GDN_W, 2 * GDN_HEADS, 2 * GDN_HEADS)
D_IN = 3 * CONV_W + 3 * NA_W + GDN_QKV + GDN_W + 4 * GDN_HEADS
N_GROUPS = 4
EXPERTS_PER_GROUP = 8
N_EXPERTS = N_GROUPS * EXPERTS_PER_GROUP
TOP_K = 2
D_EXPERT = 512
MOE_BLOCK = 256


def _rmsnorm(x, w):
    xf = x.astype(jnp.float32)
    y = xf * lax.rsqrt(jnp.mean(xf * xf, axis=-1, keepdims=True) + EPS)
    return (y * w.astype(jnp.float32)).astype(x.dtype)

def _l2norm(x):
    xf = x.astype(jnp.float32)
    return xf * lax.rsqrt(jnp.sum(xf * xf, axis=-1, keepdims=True) + EPS)

def _dwconv(x, w):
    ch = x.shape[-1]
    return lax.conv_general_dilated(x, w[:, None, :].astype(x.dtype), window_strides=(1,), padding='SAME',
                                    dimension_numbers=('NWC', 'WIO', 'NWC'), feature_group_count=ch)

def _neighbourhood_attention(q, k, v, rpb):
    bsz, t, h, dh = q.shape
    rows = t // GRID_W
    kh = min(NA_KH, rows)
    qg = q.reshape(bsz, rows, GRID_W, h, dh)
    kg = k.reshape(bsz, rows, GRID_W, h, dh)
    vg = v.reshape(bsz, rows, GRID_W, h, dh)
    col = jnp.arange(GRID_W)
    col_idx = jnp.clip(col - NA_KW // 2, 0, GRID_W - NA_KW)[:, None] + jnp.arange(NA_KW)[None, :]
    dc = col_idx - col[:, None] + (NA_KW - 1)
    row_start = jnp.clip(jnp.arange(rows) - kh // 2, 0, rows - kh)
    scale = dh ** -0.5

    def one_row(r):
        rs = row_start[r]
        q_r = lax.dynamic_index_in_dim(qg, r, axis=1, keepdims=False)
        k_rows = lax.dynamic_slice_in_dim(kg, rs, kh, axis=1)
        v_rows = lax.dynamic_slice_in_dim(vg, rs, kh, axis=1)
        k_win = k_rows[:, :, col_idx]
        v_win = v_rows[:, :, col_idx]
        dr = rs + jnp.arange(kh) - r + (NA_KH - 1)
        bias = rpb[:, dr][:, :, dc]
        s = jnp.einsum('bchd,brckhd->bhcrk', q_r, k_win).astype(jnp.float32) * scale
        s = s + jnp.transpose(bias, (0, 2, 1, 3)).astype(jnp.float32)[None]
        p = jax.nn.softmax(s.reshape(bsz, h, GRID_W, kh * NA_KW), axis=-1).reshape(s.shape).astype(v.dtype)
        return jnp.einsum('bhcrk,brckhd->bchd', p, v_win)

    out = lax.map(one_row, jnp.arange(rows))
    return jnp.transpose(out, (1, 0, 2, 3, 4)).reshape(bsz, t, h * dh)

def _gated_delta_chunked(q, k, v, g, beta):
    bsz, h, t, dk = q.shape
    dv = v.shape[-1]
    n = t // GDN_CHUNK
    cs = lambda a: a.reshape((bsz, h, n, GDN_CHUNK) + a.shape[3:])
    q, k, v, g, beta = cs(q), cs(k), cs(v), cs(g), cs(beta)
    g = jnp.cumsum(g, axis=-1)
    idx = jnp.arange(GDN_CHUNK)
    strict = idx[:, None] > idx[None, :]
    incl = idx[:, None] >= idx[None, :]
    diff = g[..., :, None] - g[..., None, :]
    dec_strict = jnp.exp(jnp.where(strict, diff, -jnp.inf))
    dec_incl = jnp.exp(jnp.where(incl, diff, -jnp.inf))
    kb = k * beta[..., None]
    lower = jnp.einsum('bhncd,bhnsd->bhncs', kb, k) * dec_strict
    rhs = jnp.concatenate([v * beta[..., None], kb * jnp.exp(g)[..., None]], axis=-1)
    sol = lax.linalg.triangular_solve(lower, rhs, left_side=True, lower=True, unit_diagonal=True)
    u, w = sol[..., :dv], sol[..., dv:]
    intra = jnp.einsum('bhncd,bhnsd->bhncs', q, k) * dec_incl
    q_dec = q * jnp.exp(g)[..., None]
    g_last = g[..., -1]
    k_dec = k * jnp.exp(g_last[..., None] - g)[..., None]

    def step(state, xs):
        u_c, w_c, intra_c, q_c, k_c, gl_c = xs
        v_new = u_c - jnp.einsum('bhcd,bhde->bhce', w_c, state)
        o_c = jnp.einsum('bhcd,bhde->bhce', q_c, state) + jnp.einsum('bhcs,bhse->bhce', intra_c, v_new)
        state = state * jnp.exp(gl_c)[..., None, None] + jnp.einsum('bhcd,bhce->bhde', k_c, v_new)
        return state, o_c

    xs = tuple(jnp.moveaxis(a, 2, 0) for a in (u, w, intra, q_dec, k_dec, g_last))
    s0 = jnp.zeros((bsz, h, dk, dv), jnp.float32)
    _, o = lax.scan(step, s0, xs)
    return jnp.moveaxis(o, 0, 2).reshape(bsz, h, t, dv)

def _gdn_mixer(qkv, z, a, b, conv_w, a_log, dt_bias, norm_w):
    bsz, t, _ = qkv.shape
    qkv = jax.nn.silu(_dwconv(qkv, conv_w))
    q = qkv[..., :GDN_HEADS * GDN_DK].reshape(bsz, t, GDN_HEADS, GDN_DK)
    k = qkv[..., GDN_HEADS * GDN_DK:2 * GDN_HEADS * GDN_DK].reshape(bsz, t, GDN_HEADS, GDN_DK)
    v = qkv[..., 2 * GDN_HEADS * GDN_DK:].reshape(bsz, t, GDN_HEADS, GDN_DV)
    q = jnp.transpose(_l2norm(q) * (GDN_DK ** -0.5), (0, 2, 1, 3))
    k = jnp.transpose(_l2norm(k), (0, 2, 1, 3))
    v = jnp.transpose(v.astype(jnp.float32), (0, 2, 1, 3))
    a = a.astype(jnp.float32).reshape(bsz, t, 2, GDN_HEADS)
    b = b.astype(jnp.float32).reshape(bsz, t, 2, GDN_HEADS)
    g = -jnp.exp(a_log.astype(jnp.float32)) * jax.nn.softplus(a + dt_bias.astype(jnp.float32))
    beta = jax.nn.sigmoid(b)
    g = jnp.transpose(g, (2, 0, 3, 1))
    beta = jnp.transpose(beta, (2, 0, 3, 1))
    flip = lambda a_: jnp.flip(a_, axis=2)
    o_fwd = _gated_delta_chunked(q, k, v, g[0], beta[0])
    o_bwd = flip(_gated_delta_chunked(flip(q), flip(k), flip(v), flip(g[1]), flip(beta[1])))
    o = jnp.transpose(o_fwd + o_bwd, (0, 2, 1, 3))
    o = o * lax.rsqrt(jnp.mean(o * o, axis=-1, keepdims=True) + EPS) * norm_w.astype(jnp.float32)
    o = o * jax.nn.silu(z.astype(jnp.float32).reshape(bsz, t, GDN_HEADS, GDN_DV))
    return o.reshape(bsz, t, GDN_W).astype(qkv.dtype)

def _hier_moe(h, wg, bg, we, be, w1, w3, w2):
    bsz, t, d = h.shape
    xt = h.reshape(bsz * t, d)
    n = xt.shape[0]
    pg = jax.nn.softmax((xt @ wg + bg).astype(jnp.float32), axis=-1)
    grp = jnp.argmax(pg, axis=-1)
    pg_top = jnp.take_along_axis(pg, grp[:, None], axis=-1)
    el = (xt @ we + be).astype(jnp.float32).reshape(n, N_GROUPS, EXPERTS_PER_GROUP)
    el_grp = jnp.take_along_axis(el, grp[:, None, None], axis=1)[:, 0]
    top_logit, top_e = lax.top_k(el_grp, TOP_K)
    gate = pg_top * jax.nn.softmax(top_logit, axis=-1)
    expert = (grp[:, None] * EXPERTS_PER_GROUP + top_e).reshape(-1)
    n_slots = n * TOP_K
    order = jnp.argsort(expert)
    sorted_e = expert[order]
    tok = order // TOP_K
    sizes = jnp.bincount(expert, length=N_EXPERTS)
    padded = (sizes + MOE_BLOCK - 1) // MOE_BLOCK * MOE_BLOCK
    pad_end = jnp.cumsum(padded)
    pad_start = pad_end - padded
    seg_start = jnp.cumsum(sizes) - sizes
    dest = pad_start[sorted_e] + jnp.arange(n_slots) - seg_start[sorted_e]
    padded_rows = (n_slots + N_EXPERTS * (MOE_BLOCK - 1) + MOE_BLOCK - 1) // MOE_BLOCK * MOE_BLOCK
    n_blocks = padded_rows // MOE_BLOCK
    buf = jnp.zeros((padded_rows, d), xt.dtype).at[dest].set(xt[tok])
    block_e = jnp.minimum(jnp.searchsorted(pad_end, jnp.arange(n_blocks) * MOE_BLOCK, side='right'), N_EXPERTS - 1)

    def expert_block(args):
        xb, e = args
        return (jax.nn.silu(xb @ w1[e]) * (xb @ w3[e])) @ w2[e]

    ys = lax.map(expert_block, (buf.reshape(n_blocks, MOE_BLOCK, d), block_e)).reshape(padded_rows, d)[dest]
    ys = ys * gate.reshape(-1)[order][:, None].astype(ys.dtype)
    return jnp.zeros_like(xt).at[tok].add(ys).reshape(bsz, t, d)

def first_inputs(seed: int = 0) -> dict:
    key = jax.random.key(seed)
    ks = jax.random.split(key, 22)
    f32 = jnp.float32
    nrm = lambda k_, shape, s: jax.random.normal(k_, shape, f32) * s
    x = nrm(ks[0], (BATCH, SEQ, D_MODEL), 1.0)
    c = nrm(ks[1], (BATCH, D_MODEL), 1.0)
    norm_mix_w = 1.0 + nrm(ks[2], (DEPTH, D_MODEL), 0.02)
    norm_ffn_w = 1.0 + nrm(ks[3], (DEPTH, D_MODEL), 0.02)
    w_ada = nrm(ks[4], (DEPTH, D_MODEL, 6 * D_MODEL), 0.5 * D_MODEL ** -0.5)
    b_ada = nrm(ks[5], (DEPTH, 6 * D_MODEL), 0.02)
    w_in = nrm(ks[6], (DEPTH, D_MODEL, D_IN), D_MODEL ** -0.5)
    conv_a_w = nrm(ks[7], (DEPTH, CONV_K, CONV_W), CONV_K ** -0.5)
    na_rpb = nrm(ks[8], (DEPTH, NA_HEADS, 2 * NA_KH - 1, 2 * NA_KW - 1), 0.1)
    gdn_conv_w = nrm(ks[9], (DEPTH, GDN_CONV_K, GDN_QKV), GDN_CONV_K ** -0.5)
    gdn_a_log = jnp.log(jax.random.uniform(ks[10], (DEPTH, 2, GDN_HEADS), f32, 1.0, 16.0))
    dt = jnp.exp(jax.random.uniform(ks[11], (DEPTH, 2, GDN_HEADS), f32, math.log(1e-3), math.log(1e-1)))
    gdn_dt_bias = dt + jnp.log(-jnp.expm1(-dt))
    gdn_norm_w = 1.0 + nrm(ks[12], (DEPTH, GDN_DV), 0.02)
    w_out = nrm(ks[13], (DEPTH, D_MIX, D_MODEL), D_MIX ** -0.5)
    router_group_w = nrm(ks[14], (DEPTH, D_MODEL, N_GROUPS), D_MODEL ** -0.5)
    router_group_b = nrm(ks[15], (DEPTH, N_GROUPS), 0.01)
    router_expert_w = nrm(ks[16], (DEPTH, D_MODEL, N_EXPERTS), D_MODEL ** -0.5)
    router_expert_b = nrm(ks[17], (DEPTH, N_EXPERTS), 0.01)
    expert_w1 = nrm(ks[18], (DEPTH, N_EXPERTS, D_MODEL, D_EXPERT), D_MODEL ** -0.5)
    expert_w3 = nrm(ks[19], (DEPTH, N_EXPERTS, D_MODEL, D_EXPERT), D_MODEL ** -0.5)
    expert_w2 = nrm(ks[20], (DEPTH, N_EXPERTS, D_EXPERT, D_MODEL), D_EXPERT ** -0.5)
    final_norm_w = 1.0 + nrm(ks[21], (D_MODEL,), 0.02)
    return {"x": x, "c": c, "norm_mix_w": norm_mix_w, "norm_ffn_w": norm_ffn_w, "w_ada": w_ada, "b_ada": b_ada,
            "w_in": w_in, "conv_a_w": conv_a_w, "na_rpb": na_rpb, "gdn_conv_w": gdn_conv_w,
            "gdn_a_log": gdn_a_log, "gdn_dt_bias": gdn_dt_bias, "gdn_norm_w": gdn_norm_w, "w_out": w_out,
            "router_group_w": router_group_w, "router_group_b": router_group_b,
            "router_expert_w": router_expert_w, "router_expert_b": router_expert_b,
            "expert_w1": expert_w1, "expert_w3": expert_w3, "expert_w2": expert_w2, "final_norm_w": final_norm_w}

def first_block(x, c, norm_mix_w, norm_ffn_w, w_ada, b_ada, w_in, conv_a_w, na_rpb, gdn_conv_w, gdn_a_log,
              gdn_dt_bias, gdn_norm_w, w_out, router_group_w, router_group_b, router_expert_w, router_expert_b,
              expert_w1, expert_w3, expert_w2, final_norm_w):
    bsz, t, _ = x.shape
    cond = jax.nn.silu(c)
    split_at = np.cumsum(IN_SPLITS)[:-1].tolist()
    for l in range(DEPTH):
        mod = cond @ w_ada[l] + b_ada[l]
        shift1, scale1, gate1, shift2, scale2, gate2 = [m[:, None, :] for m in jnp.split(mod, 6, axis=-1)]
        hmix = _rmsnorm(x, norm_mix_w[l]) * (1.0 + scale1) + shift1
        proj = hmix @ w_in[l]
        cb, cc, cx, nq, nk, nv, gqkv, gz, ga, gb = jnp.split(proj, split_at, axis=-1)
        y_conv = cb * _dwconv(cc * cx, conv_a_w[l])
        y_na = _neighbourhood_attention(nq.reshape(bsz, t, NA_HEADS, NA_DH), nk.reshape(bsz, t, NA_HEADS, NA_DH),
                                        nv.reshape(bsz, t, NA_HEADS, NA_DH), na_rpb[l])
        y_gdn = _gdn_mixer(gqkv, gz, ga, gb, gdn_conv_w[l], gdn_a_log[l], gdn_dt_bias[l], gdn_norm_w[l])
        mixed = jnp.concatenate([y_conv, y_na, y_gdn], axis=-1) @ w_out[l]
        x = x + gate1 * mixed
        hffn = _rmsnorm(x, norm_ffn_w[l]) * (1.0 + scale2) + shift2
        y_moe = _hier_moe(hffn, router_group_w[l], router_group_b[l], router_expert_w[l], router_expert_b[l],
                          expert_w1[l], expert_w3[l], expert_w2[l])
        x = x + gate2 * y_moe
    return _rmsnorm(x, final_norm_w)


CHUNK = 64
GM_BLOCK = 128
GM_GROUP_DIM = 128
GM_WIDTH = D_MODEL
GM_GROUPS = GM_WIDTH // GM_GROUP_DIM
HG_DK = 128
HG_DV = 128
HG_HEADS = D_MODEL // 128
HG_KWIDTH = HG_HEADS * HG_DK
HG_WIDTH = HG_HEADS * HG_DV
HG_CHUNK = 16
D_FF = -((-8 * D_MODEL) // (3 * 256)) * 256
PLE_DIM = 256
ALPHA = (2.0 * DEPTH) ** 0.25
BETA = (8.0 * DEPTH) ** -0.25
LN_EPS = 1e-5
RMS_EPS = 1e-6
IN_SPLITS_2 = (GM_WIDTH, GM_WIDTH, HG_KWIDTH, HG_KWIDTH, HG_WIDTH, HG_WIDTH, D_MODEL, D_MODEL)
D_IN_2 = sum(IN_SPLITS_2)
IN_OFFSETS = tuple(int(o) for o in np.cumsum(IN_SPLITS_2)[:-1])


def _layer_norm(x, g, b):
    xf = x.astype(jnp.float32)
    xc = xf - jnp.mean(xf, -1, keepdims=True)
    var = jnp.mean(xc * xc, -1, keepdims=True)
    y = xc * lax.rsqrt(var + LN_EPS) * g.astype(jnp.float32) + b.astype(jnp.float32)
    return y.astype(x.dtype)

def _rms_norm(x, g):
    return x * lax.rsqrt(jnp.mean(x * x, -1, keepdims=True) + RMS_EPS) * g

def _gmlp_spatial_gate(u, v, v_g, v_b, w_s, b_s):
    bsz, seq, _ = v.shape
    pos = jnp.arange(GM_BLOCK)
    mask = (pos[:, None] // CHUNK) >= (pos[None, :] // CHUNK)
    w = jnp.where(mask[None], w_s, jnp.zeros_like(w_s))
    vn = _layer_norm(v, v_g, v_b).reshape(bsz, seq // GM_BLOCK, GM_BLOCK, GM_GROUPS, GM_GROUP_DIM)
    mixed = jnp.einsum("gts,bnsgc->bntgc", w, vn) + b_s.T[:, :, None]
    return u * mixed.reshape(bsz, seq, GM_WIDTH)

def _hgrn2(q_raw, f_raw, i_raw, g_raw, lb, o_g):
    bsz, seq, _ = q_raw.shape
    nc = seq // HG_CHUNK
    f32 = jnp.float32

    def heads(t, d):
        return t.astype(f32).reshape(bsz, nc, HG_CHUNK, HG_HEADS, d)

    lbf = lb.astype(f32)
    fr = f_raw.astype(f32)
    log_f = heads(jnp.log(lbf + (1.0 - lbf) * jax.nn.sigmoid(fr)), HG_DK)
    k = heads((1.0 - lbf) * jax.nn.sigmoid(-fr), HG_DK)
    q = heads(jax.nn.silu(q_raw.astype(f32)), HG_DK)
    v = heads(i_raw, HG_DV)
    b = jnp.cumsum(log_f, axis=2)
    q_dec = q * jnp.exp(b)
    k_dec = k * jnp.exp(-b)
    causal = jnp.tril(jnp.ones((HG_CHUNK, HG_CHUNK), f32))
    scores = jnp.einsum("bnthd,bnshd->bnhts", q_dec, k_dec) * causal
    o_intra = jnp.einsum("bnhts,bnshe->bnthe", scores, v)
    b_last = b[:, :, -1:]
    k_end = k * jnp.exp(b_last - b)
    decay = jnp.exp(b_last[:, :, 0])

    def step(state, xs):
        qc, kc, vc, dc = xs
        o = jnp.einsum("bthd,bhde->bthe", qc, state)
        state = dc[..., None] * state + jnp.einsum("bthd,bthe->bhde", kc, vc)
        return state, o

    s0 = jnp.zeros((bsz, HG_HEADS, HG_DK, HG_DV), f32)
    _, o_inter = lax.scan(step, s0, (jnp.moveaxis(q_dec, 1, 0), jnp.moveaxis(k_end, 1, 0),
                                     jnp.moveaxis(v, 1, 0), jnp.moveaxis(decay, 1, 0)))
    o = (o_intra + jnp.moveaxis(o_inter, 0, 1)).reshape(bsz, seq, HG_HEADS, HG_DV)
    o = _rms_norm(o, o_g.astype(f32).reshape(HG_HEADS, HG_DV)).reshape(bsz, seq, HG_WIDTH)
    o = o * jax.nn.silu(g_raw.astype(f32))
    return o.astype(q_raw.dtype)

def second_inputs(seed: int = 0) -> dict:
    key = jax.random.key(seed)
    ks = jax.random.split(key, 26)
    f32 = jnp.float32
    L = DEPTH

    def nrm(k, shape, scale):
        return jax.random.normal(k, shape, f32) * scale

    def gain(k, shape):
        return 1.0 + nrm(k, shape, 0.02)

    return {
        "x": nrm(ks[0], (BATCH, SEQ, D_MODEL), 1.0),
        "p": nrm(ks[1], (DEPTH, BATCH, SEQ, PLE_DIM), 1.0),
        "ln0_g": gain(ks[2], (D_MODEL,)),
        "ln0_b": nrm(ks[3], (D_MODEL,), 0.02),
        "w_in": nrm(ks[4], (L, D_MODEL, D_IN_2), D_MODEL ** -0.5),
        "b_in": nrm(ks[5], (L, D_IN_2), 0.02),
        "gm_norm_g": gain(ks[6], (L, GM_WIDTH)),
        "gm_norm_b": nrm(ks[7], (L, GM_WIDTH), 0.02),
        "gm_w_s": nrm(ks[8], (L, GM_GROUPS, GM_BLOCK, GM_BLOCK), 0.5 * GM_BLOCK ** -0.5),
        "gm_b_s": gain(ks[9], (L, GM_GROUPS, GM_BLOCK)),
        "hg_lb_logits": nrm(ks[10], (L + 1, HG_KWIDTH), 0.5),
        "hg_norm_g": gain(ks[11], (L, HG_WIDTH)),
        "w_a": nrm(ks[12], (L, GM_WIDTH, D_MODEL), BETA * GM_WIDTH ** -0.5),
        "w_b": nrm(ks[13], (L, HG_WIDTH, D_MODEL), BETA * HG_WIDTH ** -0.5),
        "w_o": nrm(ks[14], (L, D_MODEL, D_MODEL), BETA * D_MODEL ** -0.5),
        "ln1_g": gain(ks[15], (L, D_MODEL)),
        "ln1_b": nrm(ks[16], (L, D_MODEL), 0.02),
        "w_ffn_gate": nrm(ks[17], (L, D_MODEL, D_FF), D_MODEL ** -0.5),
        "w_ffn_up": nrm(ks[18], (L, D_MODEL, D_FF), BETA * D_MODEL ** -0.5),
        "w_ffn_down": nrm(ks[19], (L, D_FF, D_MODEL), BETA * D_FF ** -0.5),
        "w_ple": nrm(ks[20], (L, PLE_DIM, D_MODEL), PLE_DIM ** -0.5),
        "w_ple_gate": nrm(ks[21], (L, D_MODEL, D_MODEL), D_MODEL ** -0.5),
        "b_ple_gate": nrm(ks[22], (L, D_MODEL), 0.02),
        "ln2_g": gain(ks[23], (L, D_MODEL)),
        "ln2_b": nrm(ks[24], (L, D_MODEL), 0.02),
    }

def second_block(x, p, ln0_g, ln0_b, w_in, b_in, gm_norm_g, gm_norm_b, gm_w_s, gm_b_s,
              hg_lb_logits, hg_norm_g, w_a, w_b, w_o, ln1_g, ln1_b,
              w_ffn_gate, w_ffn_up, w_ffn_down, w_ple, w_ple_gate, b_ple_gate, ln2_g, ln2_b):
    lb_all = jnp.cumsum(jax.nn.softmax(hg_lb_logits.astype(jnp.float32), axis=0), axis=0)
    h = _layer_norm(x, ln0_g, ln0_b)
    for i in range(DEPTH):
        proj = jnp.einsum("bsd,de->bse", h, w_in[i]) + b_in[i]
        u_r, v_r, q_r, f_r, i_r, g_r, ga_r, gb_r = jnp.split(proj, IN_OFFSETS, axis=-1)
        y_a = _gmlp_spatial_gate(jax.nn.gelu(u_r), jax.nn.gelu(v_r), gm_norm_g[i], gm_norm_b[i],
                                 gm_w_s[i], gm_b_s[i])
        y_b = _hgrn2(q_r, f_r, i_r, g_r, lb_all[i], hg_norm_g[i])
        merged = (jax.nn.sigmoid(ga_r) * jnp.einsum("bsc,cd->bsd", y_a, w_a[i])
                  + jax.nn.sigmoid(gb_r) * jnp.einsum("bsc,cd->bsd", y_b, w_b[i]))
        mix = jnp.einsum("bsd,de->bse", merged, w_o[i])
        h1 = _layer_norm(ALPHA * h + mix, ln1_g[i], ln1_b[i])
        hid = jax.nn.silu(jnp.einsum("bsd,df->bsf", h1, w_ffn_gate[i])) * jnp.einsum("bsd,df->bsf", h1, w_ffn_up[i])
        ffn = jnp.einsum("bsf,fd->bsd", hid, w_ffn_down[i])
        ple = (jax.nn.sigmoid(jnp.einsum("bsd,de->bse", h1, w_ple_gate[i]) + b_ple_gate[i])
               * jnp.einsum("bsr,rd->bsd", p[i], w_ple[i]))
        h = _layer_norm(ALPHA * h1 + ffn + ple, ln2_g[i], ln2_b[i])
    return h


_first_inputs = second_inputs


def second_inputs(seed=0):
    import zlib

    import numpy as np

    out = dict(_first_inputs(seed))
    spreads = {}
    factors = {'ln0_g': 2.943,
     'ln0_b': 3.089,
     'b_in': 8.0,
     'gm_norm_g': 64.0,
     'gm_norm_b': 64.0,
     'gm_b_s': 36.12,
     'hg_lb_logits': 8.0,
     'hg_norm_g': 36.131,
     'ln1_g': 3.045,
     'ln1_b': 3.023,
     'b_ple_gate': 64.0,
     'ln2_g': 8.438,
     'ln2_b': 8.269}
    for name, (base, spread) in spreads.items():
        noise = np.random.default_rng([zlib.crc32(name.encode()), seed]).standard_normal(out[name].shape)
        drawn = base * np.exp(spread * noise) if base else spread * noise
        out[name] = __import__('jax').numpy.asarray(drawn.astype(out[name].dtype))
    for name, factor in factors.items():
        out[name] = (out[name] * factor).astype(out[name].dtype)
    return out


_narrow_inputs = second_inputs


def second_inputs(seed=0):

    out = dict(_narrow_inputs(seed))
    wider = {'gm_norm_g': 5.77,
     'gm_norm_b': 6.02,
     'gm_b_s': 4.66,
     'hg_norm_g': 4.64,
     'ln2_g': 3.27,
     'ln2_b': 3.27}
    for name, times in wider.items():
        mean = out[name].mean()
        out[name] = (mean + times * (out[name] - mean)).astype(out[name].dtype)
    return out


HEAD_DIM = 64
V_DIM = 2 * HEAD_DIM
N_HEADS = D_MODEL // V_DIM
D_QK = 2 * N_HEADS * HEAD_DIM
D_V = N_HEADS * V_DIM
D_CONV = D_MODEL
CONV_WIDTH = 31
D_FF_3 = 4 * D_MODEL
N_BRANCH = 2
N_MOD = 6
ROPE_THETA = 10000.0
Q_BLOCK = 128
D_IN_3 = 2 * D_CONV + 2 * D_QK + D_V + N_BRANCH * D_MODEL


def rms_norm(x, g):
    xf = x.astype(jnp.float32)
    y = xf * lax.rsqrt(jnp.mean(xf * xf, axis=-1, keepdims=True) + EPS)
    return (y * g.astype(jnp.float32)).astype(x.dtype)

def layer_norm(x, g, b):
    xf = x.astype(jnp.float32)
    mu = jnp.mean(xf, axis=-1, keepdims=True)
    xc = xf - mu
    y = xc * lax.rsqrt(jnp.mean(xc * xc, axis=-1, keepdims=True) + EPS)
    return (y * g.astype(jnp.float32) + b.astype(jnp.float32)).astype(x.dtype)

def rope(x, pos):
    half = HEAD_DIM // 2
    inv_freq = ROPE_THETA ** (-jnp.arange(0, HEAD_DIM, 2, dtype=jnp.float32) / HEAD_DIM)
    ang = pos.astype(jnp.float32)[:, None] * inv_freq[None, :]
    cos = jnp.cos(ang)[None, :, None, :]
    sin = jnp.sin(ang)[None, :, None, :]
    xf = x.astype(jnp.float32)
    x1, x2 = xf[..., :half], xf[..., half:]
    return jnp.concatenate([x1 * cos - x2 * sin, x2 * cos + x1 * sin], axis=-1).astype(x.dtype)

def lambda_init(layer_idx):
    return 0.8 - 0.6 * math.exp(-0.3 * (layer_idx - 1))

def causal_diff_attention(q1, q2, k1, k2, v, lam):
    B, T, H, Dh = q1.shape
    nb = T // Q_BLOCK
    scale = 1.0 / math.sqrt(HEAD_DIM)
    kpos = jnp.arange(T)

    def to_blocks(q):
        return q.reshape(B, nb, Q_BLOCK, H, Dh).transpose(1, 0, 2, 3, 4)

    def one_block(args):
        i, qb1, qb2 = args
        qpos = i * Q_BLOCK + jnp.arange(Q_BLOCK)
        mask = kpos[None, :] <= qpos[:, None]

        def probs(qb, k):
            s = jnp.einsum('bqhd,bkhd->bhqk', qb, k, preferred_element_type=jnp.float32) * scale
            s = jnp.where(mask[None, None], s, -jnp.inf)
            return jax.nn.softmax(s, axis=-1)

        a = probs(qb1, k1) - lam * probs(qb2, k2)
        return jnp.einsum('bhqk,bkhe->bqhe', a.astype(v.dtype), v)

    out = lax.map(one_block, (jnp.arange(nb), to_blocks(q1), to_blocks(q2)))
    return out.transpose(1, 0, 2, 3, 4).reshape(B, T, H, V_DIM)

def third_inputs(seed: int = 0) -> dict:
    key = jax.random.key(seed)
    ks = jax.random.split(key, 24)
    f32 = jnp.float32
    L = DEPTH

    def nrm(k, shape, s):
        return jax.random.normal(k, shape, f32) * s

    def gain(k, shape):
        return 1.0 + 0.02 * jax.random.normal(k, shape, f32)

    return {
        "x": jax.random.normal(ks[0], (BATCH, SEQ, D_MODEL), f32),
        "c": jax.random.normal(ks[1], (BATCH, D_MODEL), f32),
        "w_ada": nrm(ks[2], (L, D_MODEL, N_MOD * D_MODEL), D_MODEL ** -0.5),
        "b_ada": nrm(ks[3], (L, N_MOD * D_MODEL), 0.01),
        "pre_norm1": gain(ks[4], (L, D_MODEL)),
        "post_norm1": gain(ks[5], (L, D_MODEL)),
        "w_in": nrm(ks[6], (L, D_MODEL, D_IN_3), D_MODEL ** -0.5),
        "conv_w": nrm(ks[7], (L, CONV_WIDTH, D_CONV), CONV_WIDTH ** -0.5),
        "conv_b": nrm(ks[8], (L, D_CONV), 0.01),
        "conv_ln_g": gain(ks[9], (L, D_CONV)),
        "conv_ln_b": nrm(ks[10], (L, D_CONV), 0.01),
        "conv_w_out": nrm(ks[11], (L, D_CONV, D_MODEL), D_CONV ** -0.5),
        "conv_b_out": nrm(ks[12], (L, D_MODEL), 0.01),
        "lambda_q1": nrm(ks[13], (L, HEAD_DIM), 0.1),
        "lambda_k1": nrm(ks[14], (L, HEAD_DIM), 0.1),
        "lambda_q2": nrm(ks[15], (L, HEAD_DIM), 0.1),
        "lambda_k2": nrm(ks[16], (L, HEAD_DIM), 0.1),
        "head_norm": gain(ks[17], (L, V_DIM)),
        "w_o": nrm(ks[18], (L, D_MODEL, D_MODEL), D_MODEL ** -0.5),
        "pre_norm2": gain(ks[19], (L, D_MODEL)),
        "post_norm2": gain(ks[20], (L, D_MODEL)),
        "w_ff1": nrm(ks[21], (L, D_MODEL, D_FF_3), D_MODEL ** -0.5),
        "w_ff2": nrm(ks[22], (L, D_FF_3, D_MODEL), D_FF_3 ** -0.5),
    }

def third_block(x, c, w_ada, b_ada, pre_norm1, post_norm1, w_in, conv_w, conv_b, conv_ln_g,
              conv_ln_b, conv_w_out, conv_b_out, lambda_q1, lambda_k1, lambda_q2, lambda_k2,
              head_norm, w_o, pre_norm2, post_norm2, w_ff1, w_ff2):
    B, T, _ = x.shape
    pos = jnp.arange(T)
    cs = jax.nn.silu(c)
    for l in range(DEPTH):
        mod = (cs @ w_ada[l] + b_ada[l])[:, None, :]
        sh1, sc1, g1, sh2, sc2, g2 = jnp.split(mod, N_MOD, axis=-1)

        h = rms_norm(x, pre_norm1[l]) * (1.0 + sc1) + sh1
        proj = h @ w_in[l]
        o1 = 2 * D_CONV
        o2 = o1 + D_QK
        o3 = o2 + D_QK
        o4 = o3 + D_V
        u_glu, q, k, v, gate_logits = proj[..., :o1], proj[..., o1:o2], proj[..., o2:o3], proj[..., o3:o4], proj[..., o4:]

        ua, ub = jnp.split(u_glu, 2, axis=-1)
        u = ua * jax.nn.sigmoid(ub)
        u = lax.conv_general_dilated(
            u, conv_w[l][:, None, :].astype(u.dtype), window_strides=(1,),
            padding=[(CONV_WIDTH - 1, 0)], dimension_numbers=('NWC', 'WIO', 'NWC'),
            feature_group_count=D_CONV) + conv_b[l]
        u = jax.nn.silu(layer_norm(u, conv_ln_g[l], conv_ln_b[l]))
        y_conv = u @ conv_w_out[l] + conv_b_out[l]

        q = q.reshape(B, T, 2, N_HEADS, HEAD_DIM)
        k = k.reshape(B, T, 2, N_HEADS, HEAD_DIM)
        v = v.reshape(B, T, N_HEADS, V_DIM)
        q1, q2 = rope(q[:, :, 0], pos), rope(q[:, :, 1], pos)
        k1, k2 = rope(k[:, :, 0], pos), rope(k[:, :, 1], pos)
        lam_init = lambda_init(l + 1)
        lam = (jnp.exp(jnp.sum(lambda_q1[l].astype(jnp.float32) * lambda_k1[l].astype(jnp.float32)))
               - jnp.exp(jnp.sum(lambda_q2[l].astype(jnp.float32) * lambda_k2[l].astype(jnp.float32)))
               + lam_init)
        att = causal_diff_attention(q1, q2, k1, k2, v, lam)
        att = rms_norm(att, head_norm[l]) * (1.0 - lam_init)
        y_att = att.reshape(B, T, D_V)

        g_conv, g_att = jnp.split(jax.nn.sigmoid(gate_logits), N_BRANCH, axis=-1)
        y = (g_conv * y_conv + g_att * y_att) @ w_o[l]
        x = x + g1 * rms_norm(y, post_norm1[l])

        h = rms_norm(x, pre_norm2[l]) * (1.0 + sc2) + sh2
        f = jnp.square(jax.nn.relu(h @ w_ff1[l])) @ w_ff2[l]
        x = x + g2 * rms_norm(f, post_norm2[l])
    return x


_first_inputs_3 = third_inputs


def third_inputs(seed=0):
    import zlib

    import numpy as np

    out = dict(_first_inputs_3(seed))
    spreads = {}
    factors = {'b_ada': 3.704,
     'pre_norm1': 5.268,
     'post_norm1': 4.935,
     'conv_b': 30.505,
     'conv_ln_g': 29.883,
     'conv_ln_b': 61.302,
     'conv_b_out': 42.071,
     'lambda_q1': 3.805,
     'lambda_k1': 5.853,
     'lambda_q2': 3.746,
     'lambda_k2': 5.252,
     'head_norm': 27.089,
     'pre_norm2': 18.689,
     'post_norm2': 24.601}
    for name, (base, spread) in spreads.items():
        noise = np.random.default_rng([zlib.crc32(name.encode()), seed]).standard_normal(out[name].shape)
        drawn = base * np.exp(spread * noise) if base else spread * noise
        out[name] = __import__('jax').numpy.asarray(drawn.astype(out[name].dtype))
    for name, factor in factors.items():
        out[name] = (out[name] * factor).astype(out[name].dtype)
    return out


_narrow_inputs_3 = third_inputs


def third_inputs(seed=0):

    out = dict(_narrow_inputs_3(seed))
    wider = {'conv_ln_g': 4.22,
     'conv_ln_b': 4.24,
     'conv_b_out': 4.23,
     'head_norm': 4.21,
     'post_norm2': 3.41}
    for name, times in wider.items():
        mean = out[name].mean()
        out[name] = (mean + times * (out[name] - mean)).astype(out[name].dtype)
    return out


def setup_inputs(seed=0):
    out = dict(first_inputs(seed))
    for name, value in second_inputs(seed + 1).items():
        if name != "x":
            out[name + "_2"] = value
    for name, value in third_inputs(seed + 2).items():
        if name != "x":
            out[name + "_3"] = value
    return out


def reference(
    x, c, norm_mix_w, norm_ffn_w, w_ada, b_ada, w_in, conv_a_w, na_rpb, gdn_conv_w, gdn_a_log,
    gdn_dt_bias, gdn_norm_w, w_out, router_group_w, router_group_b, router_expert_w,
    router_expert_b, expert_w1, expert_w3, expert_w2, final_norm_w, p_2, ln0_g_2, ln0_b_2,
    w_in_2, b_in_2, gm_norm_g_2, gm_norm_b_2, gm_w_s_2, gm_b_s_2, hg_lb_logits_2, hg_norm_g_2,
    w_a_2, w_b_2, w_o_2, ln1_g_2, ln1_b_2, w_ffn_gate_2, w_ffn_up_2, w_ffn_down_2, w_ple_2,
    w_ple_gate_2, b_ple_gate_2, ln2_g_2, ln2_b_2, c_3, w_ada_3, b_ada_3, pre_norm1_3,
    post_norm1_3, w_in_3, conv_w_3, conv_b_3, conv_ln_g_3, conv_ln_b_3, conv_w_out_3,
    conv_b_out_3, lambda_q1_3, lambda_k1_3, lambda_q2_3, lambda_k2_3, head_norm_3, w_o_3,
    pre_norm2_3, post_norm2_3, w_ff1_3, w_ff2_3,
):
    x = first_block(
        x, c, norm_mix_w, norm_ffn_w, w_ada, b_ada, w_in, conv_a_w, na_rpb, gdn_conv_w,
        gdn_a_log, gdn_dt_bias, gdn_norm_w, w_out, router_group_w, router_group_b,
        router_expert_w, router_expert_b, expert_w1, expert_w3, expert_w2, final_norm_w,
    )
    x = second_block(
        x, p_2, ln0_g_2, ln0_b_2, w_in_2, b_in_2, gm_norm_g_2, gm_norm_b_2, gm_w_s_2, gm_b_s_2,
        hg_lb_logits_2, hg_norm_g_2, w_a_2, w_b_2, w_o_2, ln1_g_2, ln1_b_2, w_ffn_gate_2,
        w_ffn_up_2, w_ffn_down_2, w_ple_2, w_ple_gate_2, b_ple_gate_2, ln2_g_2, ln2_b_2,
    )
    return third_block(
        x, c_3, w_ada_3, b_ada_3, pre_norm1_3, post_norm1_3, w_in_3, conv_w_3, conv_b_3,
        conv_ln_g_3, conv_ln_b_3, conv_w_out_3, conv_b_out_3, lambda_q1_3, lambda_k1_3,
        lambda_q2_3, lambda_k2_3, head_norm_3, w_o_3, pre_norm2_3, post_norm2_3, w_ff1_3,
        w_ff2_3,
    )


_drawn_inputs = setup_inputs


def setup_inputs(seed=0):
    import zlib

    import numpy as np

    out = dict(_drawn_inputs(seed))
    spreads = {}
    factors = {'gdn_norm_w': 2.909,
     'router_group_b': 4.058,
     'router_expert_b': 3.47,
     'post_norm1_3': 8.0,
     'conv_b_3': 2.783,
     'conv_ln_g_3': 2.692,
     'conv_b_out_3': 2.743,
     'lambda_q1_3': 8.0,
     'lambda_k1_3': 6.316,
     'head_norm_3': 3.004,
     'pre_norm2_3': 2.756}
    for name, (base, spread) in spreads.items():
        noise = np.random.default_rng([zlib.crc32(name.encode()), seed]).standard_normal(out[name].shape)
        drawn = base * np.exp(spread * noise) if base else spread * noise
        out[name] = __import__('jax').numpy.asarray(drawn.astype(out[name].dtype))
    for name, factor in factors.items():
        out[name] = (out[name] * factor).astype(out[name].dtype)
    return out
```

```python
from contextlib import ExitStack

import concourse.bass as bass
from concourse import mybir

ALU = mybir.AluOpType
ACT = mybir.ActivationFunctionType
AX_X = mybir.AxisListType.X
F32 = mybir.dt.float32
R = mybir.dt.float32r
I32 = mybir.dt.int32
U32 = mybir.dt.uint32

P = 128
T = 512
TT = T // P
D = 1024
KD = D // P
EPS = 1e-6
LN_EPS = 1e-5
BIG = 1e30

NA_H, NA_DH, GRID, NA_ROWS = 4, 64, 64, 8
RPB_H, RPB_W = 15, 31
GH, GD, GC = 4, 128, 64
GN = T // GC
N_EXP, D_EXP, EPG, N_GRP = 32, 512, 8, 4
N_SPILL = (2 * T - N_EXP) // P
N_BLK = N_EXP + N_SPILL + 1

HH, HC = 8, 16
D_FF2 = 2816
ALPHA = 2.0 ** 0.25

CONV3 = 31
D_FF3 = 4096
DIFF_H = 8
LAM_INIT = 0.2

SQUARES = ("ident", "ones", "mean", "inc_f", "inc_b", "str_f", "str_b", "near", "far", "before", "hg_causal",
           "rope_rot", "causal_add", "half_lo", "half_hi", "iota", "part",
           "hg_32", "hg_64", "hg_128")
SQ = {n: i for i, n in enumerate(SQUARES)}

VECTORS = (("c", 8), ("b_ada", 48), ("norm_mix_w", 8), ("norm_ffn_w", 8), ("final_norm_w", 8), ("conv_a_w", 6),
           ("gdn_conv_w", 36), ("gdn_norm_w", 1),
           ("ln0_g_2", 8), ("ln0_b_2", 8), ("b_in_2", 64), ("hg_lb_logits_2", 16), ("hg_norm_g_2", 8),
           ("ln1_g_2", 8), ("ln1_b_2", 8), ("b_ple_gate_2", 8), ("ln2_g_2", 8), ("ln2_b_2", 8),
           ("c_3", 8), ("b_ada_3", 48), ("pre_norm1_3", 8), ("post_norm1_3", 8), ("conv_b_3", 8),
           ("conv_ln_g_3", 8), ("conv_ln_b_3", 8), ("conv_b_out_3", 8), ("pre_norm2_3", 8),
           ("post_norm2_3", 8), ("head_norm_3", 1), ("conv_w_3", 248))
ROWS = (("gdn_a_log", 8), ("gdn_dt_bias", 8), ("router_group_b", 4), ("router_expert_b", 32),
        ("lambda_q1_3", 64), ("lambda_k1_3", 64), ("lambda_q2_3", 64), ("lambda_k2_3", 64))
ROWS2 = (("gm_norm_g_2", 1024), ("gm_norm_b_2", 1024), ("gm_b_s_2", 1024), ("b_in_2", 8192))


def placed(parts):
    at, out = 0, {}
    for name, n in parts:
        out[name] = at
        at += n
    return out, at


COL, N_COLS = placed(VECTORS)
ROW, N_ROWS = placed(ROWS)
ROW2, N_ROWS2 = placed(ROWS2)

NORMS = ("n1", "n2", "n3", "ln0", "ln1", "ln2", "pre1", "conv_ln", "post1", "pre2", "post2")
SHIFTED = ("n1", "n2", "ln0", "ln1", "ln2", "pre1", "conv_ln", "pre2")
CENTERED = ("ln0", "ln1", "ln2", "conv_ln")
COL_TILES = -(-N_COLS // P)
CHAINS = {
    "tensor_a": (("vec_turned", COL_TILES), ("na_scores", 16), ("l2_summed", 8), ("gate_sums", 1), ("kv_turned", 8),
                 ("g_rows", 8), ("scan_ks", 16), ("gdn_summed", 4), ("logits", 1), ("tok_turned", 8),
                 ("route_cum", 1), ("slot_tokens", 1), ("comb_turned", 8), ("spatial_turned", 2),
                 ("spatial_mixed", 8), ("hg_scored", 32), ("hg_summed", 8), ("p_turned", 2), ("rope_rotated", 16),
                 ("diff_scores", 32)),
    "tensor_b": (("x_turned", 16), ("na_turned", 16), ("inv_pe", 80), ("scan_y", 16), ("hg_turned", 8),
                 ("diff_turned", 32)),
    "tensor_c": (("na_mixed", 16), ("scan_o", 16), ("hg_kv", 8), ("diff_mixed", 32)),
    "tensor_d": (("scan_kv", 14), ("hg_o", 8), ("diff_back", 8)),
    "scalar_a": (("gdn_silu", 12), ("na_exp", 16), ("l2_squared", 8), ("kv_tokens", 8), ("row_exp", 8),
                 ("scan_v", 16), ("gdn_squared", 4), ("tok_copied", 8), ("v_gelu", 8), ("hg_logf", 8),
                 ("hg_exp", 64), ("hg_squared", 8), ("p_ready", 2), ("diff_exp", 64)),
    "scalar_b": (("na_probs_t", 16), ("l2_std", 8), ("gate_softplus", 3), ("gate_exp", 3), ("decay", 8),
                 ("scan_out", 16), ("gdn_std", 4), ("route_exp", 2), ("lb", 2), ("v_std", 1), ("hg_ktok", 8),
                 ("hg_std", 8), ("lam_exp", 1), ("diff_probs_t", 32)),
    "scalar_c": (("cond", 1), ("cond3", 1), ("na_out", 16), ("inv_act", 40), ("hg_out", 8), ("diff_squared", 32), ),
    "vector_a": (("small_set", 1), ("pad_zero", 1), ("vecs_ready", COL_TILES), ("x_ready", 16), ("ada_ready", 1), ("gdn_conved", 12), ("y_conv", 2), ("ada_rest", 1), ("bias_ready", 8), ("na_scored", 16), ("l2_done", 8),
                 ("gate_t", 1), ("gate_g", 1), ("gate_done", 2), ("g_diff", 8), ("scan_state", 16), ("gdn_sum", 4),
                 ("zero_rows", 1), ("route_sub", 1), ("route_diff", 1), ("route_oh", 1), ("route_place", 1),
                 ("route_done", 1), ("combined", 4), ("x_moe", 8), ("lb_diff", 2), ("spatial", 4),
                 ("v_moments", 4), ("v_normed", 4), ("spatial_added", 8), ("branch_a", 8), ("hg_f", 8),
                 ("hg_b", 16), ("merged", 8), ("ada3_ready", 1), ("lam_sums", 1), ("x_ffn2", 8),
                 ("diff_max", 32), ("merged3", 8), ("x_att", 8), ("x_done", 8)),
    "vector_b": (("na_max", 16), ("masks_done", 8), ("scan_resid", 16), ("y_gdn", 4), ("y_a", 8), ("hg_k", 8),
                 ("hg_qk", 32), ("y_b", 8), ("diff_probs", 32)),
    "vector_c": (("na_probs", 16), ("intra", 8), ("scan_vdec", 14), ("hg_d", 32), ("roped", 16), ("diff_rows", 4)),
    "vector_d": (("scan_zero", 4), ("comb_dve", 4), ("hg_kend", 8), ("u_conved", 8), ("att", 32)),
    "scalar_d": (("diff_std", 4), ("ff1_squared", D_FF3 // P)),
    "vector_e": (("inv_dve", 72), ("x0_split", 8), ("x0_moved", 8), ("x0_whole", 8), ("hg_state", 8), ("x1_split", 8), ("h3_in_split", 8), ("h3_split", 8)),
}
CHAIN_OF = {name: (chain, sum(m for _, m in links[:i])) for chain, links in CHAINS.items()
            for i, (name, _) in enumerate(links)}


class Granule:

    def __init__(self, src, kt, cols):
        self.src, self.kt, self.cols = src, kt, cols


def plan(w):
    layers, order = {}, []

    def layer(name, mat, pieces, tiles):
        view = mat.rearrange("(k p) n -> p k n", p=P)
        gs = []
        for (k0, kt, c0, nc_), n in zip(pieces, tiles):
            g = Granule(view[:, k0:k0 + kt, c0:c0 + nc_], kt, nc_)
            g.view, g.c0, g.tiles = view, c0, n
            gs.append(g)
        layers[name] = gs
        order.extend(gs)

    def cols(c0, n, step=512):
        return [(0, KD, c0 + c, min(step, n - c)) for c in range(0, n, step)]


    layer("ada", w["w_ada"], cols(0, 2 * D), [1] * 4)
    ada = 0

    def summed(name, mat, i):
        nonlocal ada
        layer(name, mat, [(0, KD, 512 * i, 512)], [1])
        layers[name][0].sum_index = ada
        ada += 1

    win = w["w_in"]
    for name, pieces, tiles in [(f"gdn_in{i}", [(0, KD, 1536 + 512 * i, 512)], 4) for i in range(3)] + [
            ("ab_in", [(0, KD, 3584, 16)], 1), ("kv_in", [(0, KD, 1024, 512)], 2 + TT),
            ("xq_in", [(0, KD, 512, 512)], 4), ("cc_in", [(0, KD, 0, 512)], 4), ("z_in", [(0, KD, 3072, 512)], 4)]:
        layer(name, win, pieces, [tiles])
        summed(f"ada{4 + ada}", w["w_ada"], 4 + ada)
    layer("out", w["w_out"], cols(0, D), [4] * 2)
    w2 = w["w_in_2"]
    layer("v2", w2, cols(1024, D), [4] * 2)
    layer("u2", w2, cols(0, D), [4] * 2)
    layer("wa2", w["w_a_2"], cols(0, D), [4] * 2)
    layer("ga2", w2, cols(6144, D), [4] * 2)
    layer("f2", w2, cols(3072, D), [4] * 2)
    layer("q2", w2, cols(2048, D), [4] * 2)
    layer("i2", w2, cols(4096, D), [4] * 2)
    layer("g2", w2, cols(5120, D), [4] * 2)
    layer("gb2", w2, cols(7168, D), [4] * 2)
    layer("wb2", w["w_b_2"], cols(0, D), [4] * 2)
    layer("wo2", w["w_o_2"], cols(0, D), [4] * 2)
    layer("pg2", w["w_ple_gate_2"], cols(0, D), [4] * 2)
    layer("ple2", w["w_ple_2"], [(0, 2, 0, D)], [8])
    gate, up = w["w_ffn_gate_2"], w["w_ffn_up_2"]
    for i in range(0, D_FF2, 512):
        n = min(512, D_FF2 - i)
        layer(f"fg{i}", gate, [(0, KD, i, n)], [n // P])
        summed(f"ada3{2 * (i // 512)}", w["w_ada_3"], 2 * (i // 512))
        layer(f"fu{i}", up, [(0, KD, i, n)], [n // P])
        summed(f"ada3{2 * (i // 512) + 1}", w["w_ada_3"], 2 * (i // 512) + 1)
    ks = [(0, 8), (8, 8), (16, 6)]
    layer("down2", w["w_ffn_down_2"], [(k, n, c, 512) for c in (0, 512) for k, n in ks], [0, 0, 4] * 2)
    w3 = w["w_in_3"]
    for i in range(2):
        layer(f"ub3{i}", w3, [(0, KD, 1024 + 512 * i, 512)], [4])
        layer(f"ua3{i}", w3, [(0, KD, 512 * i, 512)], [4])
    layer("q3", w3, cols(2048, D), [4] * 2)
    layer("k3", w3, cols(3072, D), [4] * 2)
    layer("v3", w3, cols(4096, D), [4] * 2)
    layer("cg3", w3, cols(5120, D), [4] * 2)
    layer("ag3", w3, cols(6144, D), [4] * 2)
    layer("co3", w["conv_w_out_3"], cols(0, D), [4] * 2)
    layer("wo3", w["w_o_3"], cols(0, D), [4] * 2)
    layer("ff1", w["w_ff1_3"], cols(0, D_FF3), [4] * 8)
    layer("ff2", w["w_ff2_3"], [(8 * k, 8, c, 512) for c in (0, 512) for k in range(4)], [0, 0, 0, 4] * 2)

    tile = used = 0
    for i, g in enumerate(order):
        g.index, g.slot, g.load = i, i % RING, i // RING + 1
        g.first_tile = tile
        tile += g.tiles
        used += g.tiles == 0
        g.release = ("tile_ready", tile) if g.tiles else ("partial_ready", used)
    return layers, order


RING = 4


def build(nc, w, out):
    L, order = plan(w)
    ctx = ExitStack()
    with ctx:
        sems = {}

        def sem(name):
            if name not in sems:
                sems[name] = ctx.enter_context(nc.semaphore(name))
            return sems[name]

        def signal(name):
            return sem(CHAIN_OF[name][0])

        def seen(name, value):
            chain, base = CHAIN_OF[name]
            return sem(chain), base + value

        def sb(name, shape, dt=F32):
            return ctx.enter_context(nc.sbuf_tensor(name, shape, dt))

        twins = {}

        def overlaid(name, shape, pieces, start=0):
            with ExitStack() as over:
                if start:
                    over.enter_context(nc.sbuf_tensor(f"{name}_before_parts", [P, start, shape[2]], F32))
                made, at = [], start
                for i, n in enumerate(pieces):
                    made.append((at * shape[2], n * shape[2],
                                 over.enter_context(nc.sbuf_tensor(f"{name}_parts{i}", [P, n, shape[2]], R))))
                    at += n
            t = sb(name, shape)
            twins[t.name] = made
            return t

        def parts(ap):
            for at, n, twin in twins[ap.tensor.name]:
                if at <= ap.offset < at + n:
                    return bass.AP(tensor=twin, offset=ap.offset - at, ap=[[n, P]] + [list(d) for d in ap.ap[1:]])
            raise ValueError("no parts there")

        PARTS_FROM = 16
        ring = overlaid("ring", [P, RING, KD * 512], [1] * RING)
        x = overlaid("x", [P, KD, T], [KD])
        h = overlaid("h", [P, KD, T], [KD])
        A = overlaid("A", [P, 48, T], [48 - PARTS_FROM], PARTS_FROM)
        square = sb("square", [P, len(SQUARES), P])
        vecs = sb("vecs", [P, COL_TILES * P])
        rows = sb("rows", [P, N_ROWS])
        mod = sb("mod", [P, 48])
        small = sb("small", [P, 384])
        bank = [ctx.enter_context(nc.psum_tensor(f"bank{i}", [P, 512], F32)) for i in range(8)]

        def dram(name, shape):
            return nc.dram_tensor(name, shape, F32).ap()

        rpb_pad = dram("rpb_pad", [NA_H * RPB_H, GRID, 127])
        tok_rows = dram("tok_rows", [T, D])
        slot_rows = dram("slot_rows", [N_BLK * P, D])

        def sq(name):
            return square[:, SQ[name], :]

        def col(name, j=0, n=1):
            return vecs[:, COL[name] + j:COL[name] + j + n]

        def row(name, n):
            return rows[:, ROW[name]:ROW[name] + n]

        def spread(ap, n, at=1):
            dims = [list(d) for d in ap.ap]
            return bass.AP(tensor=ap.tensor, offset=ap.offset, ap=dims[:at] + [[0, n]] + dims[at:])

        eps = small[:, 0:1]
        ln_eps = small[:, 1:2]
        zero = small[:, 2:3]
        one = small[:, 3:4]

        counts = {}

        def then(ins, name, n=1):
            ins.then_inc(signal(name) if name in CHAIN_OF else sem(name), n)
            counts[name] = counts.get(name, 0) + n
            return counts[name]

        def ordered(eng, name):
            name = f"{name.rsplit('_', 1)[1]}_order"

            def step(ins):
                eng.wait_ge(sem(name), then(ins, name))
            return step


        def weights_here(pe, g):
            pe.wait_ge(sem(f"ring_loaded{g.slot}"), 16 * g.load)

        def bank_free(pe, tile):
            if tile >= 4:
                pe.wait_ge(sem("tile_read"), tile - 3)

        def ring_tile(g):
            return ring[:, g.slot, 0:g.kt * g.cols].rearrange("p (k n) -> p k n", k=g.kt)

        def project(pe, gs, rhs):
            for g in gs:
                weights_here(pe, g)
                for m in range(g.tiles):
                    tile = g.first_tile + m
                    bank_free(pe, tile)
                    for k in range(g.kt):
                        mm = pe.matmul(bank[tile % 4][:], ring_tile(g)[:, k, m * P:(m + 1) * P], rhs(k),
                                       start=(k == 0), stop=(k == g.kt - 1))
                    mm.then_inc(sem("tile_ready"), 1)

        def project_tokens(pe, g, lhs, c0, n, first_tile):
            for t in range(TT):
                bank_free(pe, first_tile + t)
                for k in range(g.kt):
                    mm = pe.matmul(bank[(first_tile + t) % 4][:, 0:n], lhs(k, t), ring_tile(g)[:, k, c0:c0 + n],
                                   start=(k == 0), stop=(k == g.kt - 1))
                mm.then_inc(sem("tile_ready"), 1)

        def project_deep(pe, gs, rhs):
            at, k_at = 0, 0
            for g in gs:
                last = g.tiles > 0
                weights_here(pe, g)
                first_tile = g.first_tile
                for m in range(4):
                    if k_at == 0:
                        bank_free(pe, first_tile + m)
                    for k in range(g.kt):
                        mm = pe.matmul(bank[(first_tile + m) % 4][:], ring_tile(g)[:, k, m * P:(m + 1) * P],
                                       rhs(k_at + k), start=(k_at + k == 0), stop=(last and k == g.kt - 1))
                    if last:
                        mm.then_inc(sem("tile_ready"), 1)
                if not last:
                    mm.then_inc(sem("partial_ready"), 1)
                k_at = 0 if last else k_at + g.kt

        class Slice:

            def __init__(self, g, m=None, k0=None):
                self.g, self.m, self.k0 = g, m, k0
                self.first = not m and not k0
                self.free = self.before = None

            def raw(self):
                t = ring_tile(self.g)
                return t[:, :, self.m * P:(self.m + 1) * P] if self.k0 is None else t[:, self.k0:self.k0 + 2, :]

            def shaped(self, buf):
                return buf.rearrange("p (k n) -> p k n", k=self.g.kt if self.k0 is None else 2)

        split_count, used_count = [0], [0]

        def number(slices):
            for i, s in enumerate(slices):
                s.q = split_count[0]
                s.before = slices[i - 2] if i >= 2 else None
                split_count[0] += 1
            return slices

        def tile_slices(*gs):
            slices = []
            for g in gs:
                for m in range(g.tiles):
                    slices.append(Slice(g, m=m))
                    slices[-1].free = ("tile_ready", g.first_tile + m + 1)
            return number(slices)

        def deep_slices(*gs):
            slices = []
            for g in gs:
                for k0 in range(0, g.kt, 2):
                    s = Slice(g, k0=k0)
                    if k0 + 2 < g.kt:
                        used_count[0] += 1
                        s.free = ("slice_used", used_count[0])
                    else:
                        s.free = g.release
                    slices.append(s)
            return number(slices)

        def split_high(act, s, high, rhs=None, rhs_high=None):
            if s.before:
                act.wait_ge(sem(s.before.free[0]), s.before.free[1])
            if s.first:
                act.wait_ge(sem(f"ring_loaded{s.g.slot}"), 16 * s.g.load)
            if rhs is not None:
                act.activation(parts(rhs_high(s.q % 2)), rhs, ACT.Copy)
            act.activation(parts(s.shaped(high(s.q % 2))), s.raw(), ACT.Copy).then_inc(sem("split_high"), 1)

        def split_low(eng, s, high, rhs=None, rhs_high=None, rhs_low=None):
            eng.wait_ge(sem("split_high"), s.q + 1)
            if rhs is not None:
                eng.tensor_tensor(parts(rhs_low(s.q % 2)), rhs, parts(rhs_high(s.q % 2)), ALU.subtract)
            eng.tensor_tensor(parts(s.raw()), s.raw(), parts(s.shaped(high(s.q % 2))), ALU.subtract)\
                .then_inc(sem("split_low"), 1)

        def three_passes(pe, out, w_high, w_low, r_high, r_low, start, stop):
            pe.matmul(out, parts(w_high), parts(r_low), start=start, stop=False)
            pe.matmul(out, parts(w_high), parts(r_high), start=False, stop=False)
            return pe.matmul(out, parts(w_low), parts(r_high), start=False, stop=stop)

        def project_split(pe, slices, high, r_high, r_low, first=None, between=None):
            for i, s in enumerate(slices):
                g, tile = s.g, s.g.first_tile + s.m
                pe.wait_ge(sem("split_low"), s.q + 1)
                bank_free(pe, tile)
                w_high = s.shaped(high(s.q % 2))
                for k in range(g.kt):
                    if i == 0 and first:
                        first(k)
                    mm = three_passes(pe, bank[tile % 4][:], w_high[:, k, :], s.raw()[:, k, :], r_high(k), r_low(k),
                                      k == 0, k == g.kt - 1)
                    if k == 1 and between:
                        between()
                mm.then_inc(sem("tile_ready"), 1)

        def project_tokens_split(pe, slices, high, l_high, l_low, first):
            for i, s in enumerate(slices):
                g = s.g
                ends = s.k0 + 2 == g.kt
                pe.wait_ge(sem("split_low"), s.q + 1)
                for t in range(TT):
                    if s.k0 == 0:
                        bank_free(pe, g.first_tile + t)
                    c = slice(t * P, (t + 1) * P)
                    for k in range(2):
                        if g is slices[0].g and t == 0:
                            first(s.k0 + k)
                        mm = three_passes(pe, bank[(g.first_tile + t) % 4][:], l_high(s.k0 + k)[:, c],
                                          l_low(s.k0 + k)[:, c], s.shaped(high(s.q % 2))[:, k, :], s.raw()[:, k, :],
                                          s.k0 + k == 0, s.k0 + k == g.kt - 1)
                    if ends:
                        mm.then_inc(sem("tile_ready"), 1)
                if not ends:
                    mm.then_inc(sem(s.free[0]), 1)

        def project_deep_split(pe, slices, high, r_high, r_low):
            start = True
            for s in slices:
                g = s.g
                ends = g.tiles > 0 and s.k0 + 2 == g.kt
                pe.wait_ge(sem("split_low"), s.q + 1)
                for m in range(4):
                    if start:
                        bank_free(pe, g.first_tile + m)
                    c = slice(m * P, (m + 1) * P)
                    for k in range(2):
                        t = slice(k * T, (k + 1) * T)
                        mm = three_passes(pe, bank[(g.first_tile + m) % 4][:], s.shaped(high(s.q % 2))[:, k, c],
                                          s.raw()[:, k, c], r_high(s.q % 2)[:, t], r_low(s.q % 2)[:, t],
                                          start and k == 0, ends and k == 1)
                    if ends:
                        mm.then_inc(sem("tile_ready"), 1)
                if not ends:
                    mm.then_inc(sem(s.free[0]), 1)
                start = ends

        def read_tile(eng, tile, first=False):
            eng.wait_ge(sem("tile_ready"), tile + 1)
            if first and tile:
                eng.wait_ge(sem("tile_read"), tile)
            return bank[tile % 4]

        def tiles_of(*gs):
            return [g.first_tile + m for g in gs for m in range(g.tiles)]

        def norm_at(n, what, v):
            shifted = [m for m in NORMS if m in SHIFTED]
            centered = [m for m in NORMS if m in CENTERED]
            among, per = {"squared": (NORMS, KD), "summed": (NORMS, KD), "std": (NORMS, 1), "rstd": (NORMS, 1),
                          "scaled": (NORMS, KD), "out": (shifted, KD), "mean": (centered, 1),
                          "centered": (centered, KD)}[what]
            return sem(f"norm_{what}"), among.index(n) * per + v

        def norm_pe(pe, n, src, squares, ready=()):
            if n in CENTERED:
                for s, v in ready:
                    pe.wait_ge(s, v)
                for k in range(KD):
                    mm = pe.matmul(bank[5][:], sq("mean"), src(k), start=(k == 0), stop=(k == KD - 1))
                mm.then_inc(sem("norm_mean"), 1)
            for k in range(KD):
                pe.wait_ge(*norm_at(n, "squared", k + 1))
                pe.matmul(bank[4][:], sq("mean"), squares(k % 2), start=(k == 0),
                          stop=(k == KD - 1)).then_inc(sem("norm_summed"), 1)

        def norm_act(act, n, src, squares, rstd, e, shift=None, dst=None, ready=(), func=ACT.Identity):
            for s, v in ready:
                act.wait_ge(s, v)
            for k in range(KD):
                if n in CENTERED:
                    act.wait_ge(*norm_at(n, "centered", k + 1))
                if k >= 2:
                    act.wait_ge(*norm_at(n, "summed", k - 1))
                act.activation(squares(k % 2), src(k), ACT.Square).then_inc(sem("norm_squared"), 1)
            act.wait_ge(*norm_at(n, "summed", KD))
            act.activation(rstd, bank[4][:], ACT.Sqrt, bias=e).then_inc(sem("norm_std"), 1)
            if n in SHIFTED:
                for k in range(KD):
                    act.wait_ge(*norm_at(n, "scaled", k + 1))
                    act.activation(dst(k), dst(k), func, bias=shift(k)).then_inc(sem("norm_out"), 1)

        def norm_dve(dve, n, src, rstd, gain, dst, xc=None, ready=()):
            for s, v in ready:
                dve.wait_ge(s, v)
            if n in CENTERED:
                dve.wait_ge(*norm_at(n, "mean", 1))
                for k in range(KD):
                    dve.tensor_tensor(xc(k), src(k), bank[5][:], ALU.subtract).then_inc(sem("norm_centered"), 1)
            dve.wait_ge(*norm_at(n, "std", 1))
            dve.reciprocal(rstd, rstd).then_inc(sem("norm_rstd"), 1)
            dve.wait_ge(*norm_at(n, "rstd", 1))
            for k in range(KD):
                dve.scalar_tensor_tensor(dst(k), xc(k) if n in CENTERED else src(k), gain(k), rstd, ALU.mult,
                                         ALU.mult).then_inc(sem("norm_scaled"), 1)

        X = lambda k: x[:, k, :]
        Hn = lambda k: h[:, k, :]
        W = lambda i: A[:, i, :]

        nv = A[:, 10:12, :].rearrange("p a (b n) -> p (a b) n", b=2)
        bias = A[:, 36:44, :].rearrange("p a n -> p (a n)").rearrange("p (h n) -> p h n", h=NA_H)
        ab = small[:, 16:80].rearrange("p (t n) -> p t n", t=TT)
        pad_tile = A[:, 45, 0:127]
        window = A[:, 46, 0:64]
        mod_raw = small[:, 336:384]

        def setup_act(act):
            act.dma_start(square[:, :, :], w["squares"].rearrange("s p n -> p s n")).then_inc(sem("squares_in"), 16)
            full = N_COLS // P
            act.dma_start(W(8).rearrange("p (b n) -> p b n", b=full),
                          w["vectors"][0:P * full, :].rearrange("(b p) n -> p b n", p=P)).then_inc(sem("vectors_in"), 16)
            rest = N_COLS - P * full
            act.dma_start(A[0:rest, 8 + full // 4, 0:P], w["vectors"][P * full:N_COLS, :]).then_inc(sem("vectors_in"), 16)
            act.dma_start(rows[:, :], w["rows"].partition_broadcast(P)).then_inc(sem("rows_in"), 16)
            act.dma_start(window[0:64, :], w["window"]).then_inc(sem("window_in"), 16)
            act.dma_start(window[64:128, :], w["window"]).then_inc(sem("window_in"), 16)
            act.wait_ge(*seen("pad_zero", 1))
            act.dma_start(pad_tile[0:NA_H * RPB_H, 48:48 + RPB_W],
                          w["na_rpb"].rearrange("h a b -> (h a) b")).then_inc(sem("rpb_in"), 16)
            act.wait_ge(sem("rpb_in"), 16)
            act.dma_start(rpb_pad, spread(pad_tile[0:NA_H * RPB_H, :], GRID)).then_inc(sem("rpb_out"), 16)
            act.wait_ge(*seen("vecs_ready", COL_TILES))
            act.activation(small[:, 4:12], col("c", 0, 8), ACT.Silu).then_inc(signal("cond"), 1)
            act.activation(small[:, 86:94], col("c_3", 0, 8), ACT.Silu).then_inc(signal("cond3"), 1)

        def bias_act(act):
            act.wait_ge(sem("rpb_out"), 16)
            for i in range(NA_H):
                for half in range(2):
                    diag = bass.AP(tensor=rpb_pad.tensor, offset=rpb_pad.offset + i * RPB_H * GRID * 127 + 63,
                                   ap=[[126, GRID], [GRID * 127, RPB_H], [1, GRID]])
                    dst = bias[64 * half:64 * half + 64, i, 64 * half:64 * half + RPB_H * GRID]
                    act.dma_start(dst.rearrange("p (a n) -> p a n", n=GRID), diag).then_inc(sem("bias_in"), 16)

        def setup_dve(dve):
            dve.memset(eps, EPS)
            dve.memset(ln_eps, LN_EPS)
            dve.memset(zero, 0.0)
            dve.memset(one, 1.0).then_inc(signal("small_set"), 1)
            dve.memset(pad_tile, 0.0).then_inc(signal("pad_zero"), 1)
            for i in range(COL_TILES):
                n = min(P, N_COLS - i * P)
                dve.wait_ge(*seen("vec_turned", i + 1))
                dve.tensor_copy(vecs[:, i * P:i * P + n], bank[4 + i % 2][:, 0:n]).then_inc(signal("vecs_ready"), 1)
            for i in range(2 * KD):
                k, half = i // 2, i % 2
                dve.wait_ge(*seen("x_turned", i + 1))
                dve.tensor_copy(x[:, k, 256 * half:256 * half + 256],
                                bank[6 + i % 2][:, 0:256]).then_inc(signal("x_ready"), 1)

        def bias_dve(dve):
            dve.wait_ge(sem("bias_in"), 16 * 2 * NA_H)
            dve.wait_ge(sem("window_in"), 32)
            for half in range(2):
                b = bias[64 * half:64 * half + 64, :, 64 * half:64 * half + RPB_H * GRID]
                for i in range(NA_H):
                    bi = b[:, i, :].rearrange("p (a n) -> p a n", n=GRID)
                    dve.tensor_tensor(bi, bi, spread(window[64 * half:64 * half + 64, :], RPB_H), ALU.add)\
                        .then_inc(signal("bias_ready"), 1)

        def setup_pe(pe):
            pe.wait_ge(sem("squares_in"), 16)
            pe.wait_ge(sem("vectors_in"), 32)
            for i in range(COL_TILES):
                n = min(P, N_COLS - i * P)
                if i >= 2:
                    pe.wait_ge(*seen("vecs_ready", i - 1))
                src = A[0:n, 8 + i // 4, (i % 4) * P:(i % 4) * P + P]
                pe.transpose(bank[4 + i % 2][:, 0:n], src, square[0:n, SQ["ident"], 0:n])\
                    .then_inc(signal("vec_turned"), 1)
            pe.wait_ge(sem("x_in"), 16)
            xt = A[:, 0:8, :].rearrange("p (t a) n -> p t (a n)", t=TT)
            for i in range(2 * KD):
                k, half = i // 2, i % 2
                if i >= 2:
                    pe.wait_ge(*seen("x_ready", i - 1))
                for t in range(2):
                    mm = pe.transpose(bank[6 + i % 2][:, t * P:(t + 1) * P],
                                      xt[:, 2 * half + t, k * P:(k + 1) * P], sq("ident"))
                mm.then_inc(signal("x_turned"), 1)

        def ada_pe(pe, gs, cond, ready):
            pe.wait_ge(*seen(ready, 1))
            for g in gs:
                weights_here(pe, g)
                bank_free(pe, g.first_tile)
                for m in range(4):
                    for k in range(KD):
                        mm = pe.matmul(bank[g.first_tile % 4][:, m:m + 1], ring_tile(g)[:, k, m * P:(m + 1) * P],
                                       cond[:, k:k + 1], start=(k == 0), stop=(k == KD - 1))
                mm.then_inc(sem("tile_ready"), 1)

        def sum_pool(pool, gs, cond, ready):
            pool.wait_ge(*seen(ready, 1))
            for g in gs:
                pool.wait_ge(sem(f"ring_loaded{g.slot}"), 16 * g.load)
                t = ring_tile(g)
                ins = pool.tensor_tensor(t, t, spread(cond, 512, at=2), ALU.mult)
                for n in (4, 2, 1):
                    then(ins, "ada_partial")
                    pool.wait_ge(sem("ada_partial"), counts["ada_partial"])
                    ins = pool.tensor_tensor(t[:, 0:n, :], t[:, 0:n, :], t[:, n:2 * n, :], ALU.add)
                ins.then_inc(sem("ada_summed"), 1)

        def sum_pe(pe, g):
            pe.wait_ge(sem("ada_summed"), g.sum_index + 1)
            bank_free(pe, g.first_tile)
            for m in range(4):
                mm = pe.matmul(bank[g.first_tile % 4][:, m:m + 1], ring_tile(g)[:, 0, m * P:(m + 1) * P],
                               sq("ones")[:, 0:1], start=True, stop=True)
            mm.then_inc(sem("tile_ready"), 1)

        def ada_act(act, g, first=False):
            b = read_tile(act, g.first_tile, first)
            j = 4 * (g.c0 // 512)
            act.activation(mod_raw[:, j:j + 4], b[:, 0:4], ACT.Copy).then_inc(sem("tile_read"), 1)

        def ada_dve(dve, g, c0, c1, b, norms, name):
            step = ordered(dve, f"{name}_dve")
            dve.wait_ge(sem("tile_read"), g.first_tile + 1)
            step(dve.tensor_tensor(mod[:, c0:c1], mod_raw[:, c0:c1], b[:, c0:c1], ALU.add))
            for i, norm in norms:
                s = mod[:, 24 * i + 8:24 * i + 16]
                ins = dve.scalar_tensor_tensor(s, s, 1.0, norm, ALU.add, ALU.mult)
            then(ins, name)
            dve.wait_ge(*seen(name, 1))

        gdn_tiles = tiles_of(*(L[f"gdn_in{i}"][0] for i in range(3)))

        def in_pe(pe):
            pe.wait_ge(*norm_at("n1", "out", KD))
            for i in range(3):
                project(pe, L[f"gdn_in{i}"], Hn)
                sum_pe(pe, L[f"ada{4 + i}"][0])
            g = L["ab_in"][0]
            weights_here(pe, g)
            bank_free(pe, g.first_tile)
            for t in range(TT):
                for k in range(KD):
                    mm = pe.matmul(bank[g.first_tile % 4][:, 16 * t:16 * t + 16], Hn(k)[:, t * P:(t + 1) * P],
                                   ring_tile(g)[:, k, :], start=(k == 0), stop=(k == KD - 1))
            mm.then_inc(sem("tile_ready"), 1)
            sum_pe(pe, L["ada7"][0])
            g = L["kv_in"][0]
            for m in range(2):
                tile = g.first_tile + m
                weights_here(pe, g)
                bank_free(pe, tile)
                for k in range(KD):
                    mm = pe.matmul(bank[tile % 4][:], ring_tile(g)[:, k, m * P:(m + 1) * P], Hn(k),
                                   start=(k == 0), stop=(k == KD - 1))
                mm.then_inc(sem("tile_ready"), 1)
            project_tokens(pe, g, lambda k, t: Hn(k)[:, t * P:(t + 1) * P], 256, 256, g.first_tile + 2)
            for i, name in enumerate(("xq_in", "cc_in", "z_in")):
                sum_pe(pe, L[f"ada{8 + i}"][0])
                project(pe, L[name], Hn)
            sum_pe(pe, L["ada11"][0])

        def in_act(act):
            def silu(j):
                act.wait_ge(*seen("gdn_conved", j + 1))
                act.activation(W(12 + j), W(44 + j % 2), ACT.Silu).then_inc(signal("gdn_silu"), 1)

            for j, tile in enumerate(gdn_tiles):
                b = read_tile(act, tile, j == 0)
                act.activation(W(12 + j), b[:], ACT.Copy).then_inc(sem("tile_read"), 1)
                if j % 4 == 3:
                    ada_act(act, L[f"ada{4 + j // 4}"][0])
                if j:
                    silu(j - 1)
            silu(11)
            b = read_tile(act, L["ab_in"][0].first_tile)
            act.activation(small[:, 16:80], b[:, 0:64], ACT.Copy).then_inc(sem("tile_read"), 1)
            ada_act(act, L["ada7"][0])
            tile = L["kv_in"][0].first_tile
            for m in range(2):
                b = read_tile(act, tile + m)
                act.activation(W(8 + m), b[:], ACT.Copy).then_inc(sem("tile_read"), 1)
            for t in range(TT):
                b = read_tile(act, tile + 2 + t)
                act.activation(nv[:, t, :], b[:, 0:256], ACT.Copy).then_inc(sem("tile_read"), 1)
            for i, (dst, tile) in enumerate(zip((4, 5, 6, 7, 0, 1, 2, 3), tiles_of(*L["xq_in"], *L["cc_in"]))):
                if i % 4 == 0:
                    ada_act(act, L[f"ada{8 + i // 4}"][0])
                b = read_tile(act, tile)
                act.activation(W(dst), b[:], ACT.Copy).then_inc(sem("tile_read"), 1)
            ada_act(act, L["ada10"][0])
            for j, tile in enumerate(tiles_of(*L["z_in"])):
                b = read_tile(act, tile)
                act.activation(W(24 + j), b[:], ACT.Silu).then_inc(sem("tile_read"), 1)
            ada_act(act, L["ada11"][0])

        def conv3(dve, step, dst, src, taps):
            step(dve.tensor_scalar(dst, src, taps(1), None, ALU.mult))
            step(dve.scalar_tensor_tensor(dst[:, 1:T], src[:, 0:T - 1], taps(0), dst[:, 1:T], ALU.mult, ALU.add))
            return dve.scalar_tensor_tensor(dst[:, 0:T - 1], src[:, 1:T], taps(2), dst[:, 0:T - 1], ALU.mult, ALU.add)

        def in_dve(dve):
            step = ordered(dve, "conv_dve")
            dve.wait_ge(sem("rpb_out"), 16)
            for j, tile in enumerate(gdn_tiles):
                dve.wait_ge(sem("tile_read"), tile + 1)
                if j >= 2:
                    dve.wait_ge(*seen("gdn_silu", j - 1))
                conv3(dve, step, W(44 + j % 2), W(12 + j),
                      lambda i, j=j: col("gdn_conv_w", 12 * i + j)).then_inc(signal("gdn_conved"), 1)
            dve.wait_ge(*seen("gdn_silu", 12))
            dve.wait_ge(sem("tile_read"), L["cc_in"][0].first_tile + 4)
            for j in range(2):
                step(dve.tensor_tensor(W(2 + j), W(2 + j), W(4 + j), ALU.mult))
                step(conv3(dve, step, W(44), W(2 + j), lambda i, j=j: col("conv_a_w", 2 * i + j)))
                then(dve.tensor_tensor(W(j), W(j), W(44), ALU.mult), "y_conv")
                dve.wait_ge(*seen("y_conv", j + 1))
            ada_dve(dve, L["ada11"][0], 16, 48, col("b_ada", 0, 48), ((1, col("norm_ffn_w", 0, 8)),), "ada_rest")

        units = [(i, q) for i in range(NA_H) for q in range(TT)]

        def na_pe(pe):
            def scores(u):
                i, q = units[u]
                r = 64 * (i % 2)
                if u >= 2:
                    pe.wait_ge(*seen("na_scored", u - 1))
                pe.matmul(bank[4 + u % 2][:], W(6 + i // 2)[r:r + 64, q * P:(q + 1) * P], W(8 + i // 2)[r:r + 64, :],
                          start=True, stop=True).then_inc(signal("na_scores"), 1)

            def turn(u):
                pe.wait_ge(*seen("na_probs", u + 1))
                if u:
                    pe.wait_ge(*seen("na_probs_t", u))
                for k in range(TT):
                    mm = pe.transpose(bank[6][:, k * P:(k + 1) * P], W(30 + u % 2)[:, k * P:(k + 1) * P], sq("ident"))
                mm.then_inc(signal("na_turned"), 1)

            def mix(u):
                i, q = units[u]
                pe.wait_ge(*seen("na_probs_t", u + 1))
                r = 64 * (i % 2)
                if u >= 2:
                    pe.wait_ge(*seen("na_out", u - 1))
                for k in range(TT):
                    mm = pe.matmul(bank[7 * (1 - u % 2)][r:r + 64, 0:P], nv[:, k, 64 * i:64 * i + 64],
                                   W(32 + u % 2)[:, k * P:(k + 1) * P], start=(k == 0), stop=(k == TT - 1))
                mm.then_inc(signal("na_mixed"), 1)

            pe.wait_ge(sem("tile_read"), L["ada11"][0].first_tile + 1)
            scores(0)
            scores(1)
            for u in range(len(units)):
                if u + 2 < len(units):
                    scores(u + 2)
                turn(u)
                if u:
                    mix(u - 1)
            mix(len(units) - 1)

        def na_dve(dve):
            step = ordered(dve, "na_dve")

            def normalise(u):
                rsum = small[:, 84 + u % 2:85 + u % 2]
                dve.wait_ge(*seen("na_exp", u + 1))
                step(dve.reciprocal(rsum, rsum))
                dve.tensor_scalar(W(30 + u % 2), W(30 + u % 2), rsum, None, ALU.mult).then_inc(signal("na_probs"), 1)

            dve.wait_ge(*seen("bias_ready", 2 * NA_H))
            for u, (i, q) in enumerate(units):
                dve.wait_ge(*seen("na_scores", u + 1))
                if u >= 2:
                    dve.wait_ge(*seen("na_exp", u - 1))
                s = W(28 + u % 2)
                at = (7 - 2 * q) * GRID
                then(dve.scalar_tensor_tensor(s, bank[4 + u % 2][:], NA_DH ** -0.5, bias[:, i, at:at + T],
                                              ALU.mult, ALU.add), "na_scored")
                dve.wait_ge(*seen("na_scored", u + 1))
                dve.tensor_reduce(small[:, 82 + u % 2:83 + u % 2], s, AX_X, ALU.max, negate=True)\
                    .then_inc(signal("na_max"), 1)
                if u:
                    normalise(u - 1)
            normalise(len(units) - 1)

        def na_act(act):
            act.wait_ge(*seen("y_conv", 2))

            def evacuate(u):
                i, q = units[u]
                r = 64 * (i % 2)
                act.wait_ge(*seen("na_mixed", u + 1))
                act.activation(W(2 + i // 2)[r:r + 64, q * P:(q + 1) * P], bank[7 * (1 - u % 2)][r:r + 64, 0:P],
                               ACT.Copy).then_inc(signal("na_out"), 1)

            for u in range(len(units)):
                act.wait_ge(*seen("na_max", u + 1))
                if u >= 2:
                    act.wait_ge(*seen("na_turned", u - 1))
                act.activation(W(30 + u % 2), W(28 + u % 2), ACT.Exp, bias=small[:, 82 + u % 2:83 + u % 2],
                               accum_out=small[:, 84 + u % 2:85 + u % 2]).then_inc(signal("na_exp"), 1)
                if u:
                    act.wait_ge(*seen("na_turned", u))
                    act.activation(W(32 + (u - 1) % 2), bank[6][:], ACT.Copy).then_inc(signal("na_probs_t"), 1)
                if u >= 2:
                    evacuate(u - 2)
            u = len(units)
            act.wait_ge(*seen("na_turned", u))
            act.activation(W(32 + (u - 1) % 2), bank[6][:], ACT.Copy).then_inc(signal("na_probs_t"), 1)
            evacuate(u - 2)
            evacuate(u - 1)

        g_ = small[:, 96:128].rearrange("p (t n) -> p t n", t=TT)
        beta = small[:, 128:160].rearrange("p (t n) -> p t n", t=TT)
        g_cum = small[:, 160:192].rearrange("p (t n) -> p t n", t=TT)
        neg_eg = small[:, 192:224].rearrange("p (t n) -> p t n", t=TT)
        beta_rest = small[:, 224:256].rearrange("p (t n) -> p t n", t=TT)
        eg_last = small[:, 256:320].rearrange("p (c n) -> p c n", c=GN)
        tmp = A[:, 47, :]
        INC, STR = ("inc_f", "inc_b"), ("str_f", "str_b")

        def scratch(d, i):
            return ring[:, 2 + d, i * T:(i + 1) * T]

        S_FAR, S_NEAR, S_NEAR_T, S_B, S_2, S_2T, S_4, S_4T = range(8)

        def heads(ap):
            return ap.rearrange("p (h n) -> p h n", h=GH)

        def head(ap, i):
            return ap[:, i * P:(i + 1) * P]

        def gdn_norm_pe(pe):
            for j in range(2 * GH):
                pe.wait_ge(*seen("l2_squared", j + 1))
                if j >= 2:
                    pe.wait_ge(*seen("l2_std", j - 1))
                pe.matmul(bank[4 + j % 2][:], sq("ones"), W(44 + j % 2), start=True, stop=True)\
                    .then_inc(signal("l2_summed"), 1)

        def gdn_norm_act(act):
            act.wait_ge(*seen("y_conv", 2))

            def std(j):
                act.wait_ge(*seen("l2_summed", j + 1))
                if j >= 2:
                    act.wait_ge(*seen("l2_done", j - 1))
                act.activation(W(20 + 10 + j % 2), bank[4 + j % 2][:], ACT.Sqrt, bias=eps).then_inc(signal("l2_std"), 1)

            for j in range(2 * GH):
                if j >= 2:
                    act.wait_ge(*seen("l2_summed", j - 1))
                act.activation(W(44 + j % 2), W(12 + j), ACT.Square).then_inc(signal("l2_squared"), 1)
                if j:
                    std(j - 1)
            std(2 * GH - 1)

        def gdn_norm_dve(dve):
            step = ordered(dve, "l2_dve")
            for j in range(2 * GH):
                r = W(30 + j % 2)
                dve.wait_ge(*seen("l2_std", j + 1))
                step(dve.reciprocal(r, r))
                dve.scalar_tensor_tensor(W(12 + j), W(12 + j), GD ** -0.5 if j < GH else 1.0, r, ALU.mult,
                                         ALU.mult).then_inc(signal("l2_done"), 1)

        def gdn_gates_act(act):
            sp = tmp[:, 32:64]
            act.wait_ge(sem("rows_in"), 16)
            act.wait_ge(*seen("gate_t", 1))
            step = ordered(act, "gate_act")
            step(act.activation(sp, tmp[:, 0:32], ACT.Abs))
            step(act.activation(sp, sp, ACT.Exp, scale=-1.0))
            act.activation(sp, sp, ACT.Ln, bias=one).then_inc(signal("gate_softplus"), 1)
            act.activation(tmp[:, 64:72], row("gdn_a_log", 8), ACT.Exp).then_inc(signal("gate_softplus"), 1)
            act.activation(beta, ab[:, :, 8:16], ACT.Sigmoid).then_inc(signal("gate_softplus"), 1)
            act.wait_ge(*seen("gate_sums", 1))
            act.activation(small[:, 160:192], bank[4][:, 0:32], ACT.Copy).then_inc(signal("gate_exp"), 1)
            act.activation(tmp[:, 96:160], bank[4][:, 0:64], ACT.Exp).then_inc(signal("gate_exp"), 1)
            act.activation(small[:, 256:320], bank[4][:, 64:128], ACT.Exp).then_inc(signal("gate_exp"), 1)

        def gdn_gates_dve(dve):
            step = ordered(dve, "gate_dve")
            t = tmp[:, 0:32]
            dve.wait_ge(sem("rows_in"), 16)
            then(dve.tensor_tensor(t.rearrange("p (t n) -> p t n", t=TT), ab[:, :, 0:8],
                                   spread(row("gdn_dt_bias", 8), TT), ALU.add), "gate_t")
            dve.wait_ge(*seen("gate_softplus", 3))
            step(dve.scalar_tensor_tensor(t, t, 0.0, tmp[:, 32:64], ALU.max, ALU.add))
            dve.scalar_tensor_tensor(g_, t.rearrange("p (t n) -> p t n", t=TT), -1.0, spread(tmp[:, 64:72], TT),
                                     ALU.mult, ALU.mult).then_inc(signal("gate_g"), 1)
            dve.wait_ge(*seen("gate_exp", 3))
            dve.tensor_scalar(small[:, 192:224], tmp[:, 96:128], -1.0, None, ALU.mult).then_inc(signal("gate_done"), 1)
            dve.tensor_tensor(small[:, 224:256], tmp[:, 128:160], small[:, 128:160], ALU.mult)\
                .then_inc(signal("gate_done"), 1)

        def gdn_gates_pe(pe):
            pe.wait_ge(*seen("gate_g", 1))
            pe.wait_ge(*seen("l2_std", 2 * GH))
            for b in range(TT):
                for d in range(2):
                    at = 8 * b + 4 * d
                    g4 = g_[:, b, 4 * d:4 * d + 4]
                    pe.matmul(bank[4][:, at:at + 4], sq(INC[d]), g4, start=True, stop=True)
                    pe.matmul(bank[4][:, 32 + at:36 + at], sq(STR[1 - d]), g4, start=True, stop=True)
            for n in range(GN):
                mm = pe.matmul(bank[4][:, 64 + 8 * n:72 + 8 * n], sq("half_hi" if n % 2 else "half_lo"),
                               g_[:, n // 2, :], start=True, stop=True)
            mm.then_inc(signal("gate_sums"), 1)

        def gdn_turn_pe(pe):
            pe.wait_ge(*seen("l2_done", 2 * GH))
            for i in range(2 * TT):
                src, b = (16, 20)[i // TT], i % TT
                if i >= 2:
                    pe.wait_ge(*seen("kv_tokens", i - 1))
                for j in range(GH):
                    mm = pe.transpose(head(bank[6 + i % 2][:], j), W(src + j)[:, b * P:(b + 1) * P], sq("ident"))
                mm.then_inc(signal("kv_turned"), 1)

        def gdn_turn_act(act):
            act.wait_ge(*seen("l2_done", 2 * GH))
            for i in range(2 * TT):
                act.wait_ge(*seen("kv_turned", i + 1))
                act.activation(W(28 + i), bank[6 + i % 2][:], ACT.Copy).then_inc(signal("kv_tokens"), 1)

        INV_DVE = (0, 1, 2, 3, 4, 4, 5, 6, 7, 8, 9)
        INV_ACT = (0, 0, 1, 2, 3, 4, 4, 5, 5, 5, 5)

        def inv_pe_at(b, d, k):
            return 2 * (10 * b + k) - (1 - d)

        def inv_dve_at(b, d, k):
            return 2 * (9 * b + INV_DVE[k]) - (1 - d)

        def inv_act_at(b, d, k):
            return 2 * (5 * b + INV_ACT[k]) - (1 - d)

        def gdn_masks_pe(pe, b):
            if b:
                pe.wait_ge(*seen("masks_done", 2 * b))
                pe.wait_ge(*seen("row_exp", 2 * b))
            c = slice(b * P, (b + 1) * P)
            for j in range(GH):
                pe.matmul(head(bank[0][:], j), W(16 + j)[:, c], W(16 + j)[:, c], start=True, stop=True)
                pe.matmul(head(bank[1][:], j), W(16 + j)[:, c], W(12 + j)[:, c], start=True, stop=True)
            for d in range(2):
                for j in range(GH):
                    gc = g_[:, b, 4 * d + j:4 * d + j + 1]
                    mm = pe.matmul(head(bank[2 + d][:], j), gc.broadcast_to([P, P]), sq(INC[d]),
                                   start=True, stop=True)
                mm.then_inc(signal("g_rows"), 1)

        def gdn_masks_dve(dve, b, d, step):
            n = 2 * b + d
            diff, e_row, incl, far, near = W(44 + d), W(20 + d), W(22 + d), scratch(d, S_FAR), scratch(d, S_NEAR)
            b4 = lambda ap: spread(ap[:, b, 4 * d:4 * d + 4], P, at=2)
            dve.wait_ge(*seen("g_rows", n + 1))
            step(dve.tensor_tensor(heads(diff), heads(bank[2 + d][:]), b4(g_cum), ALU.subtract))
            then(dve.tensor_scalar(diff, diff, 0.0, None, ALU.min), "g_diff")
            dve.wait_ge(*seen("decay", n + 1))
            step(dve.tensor_tensor(heads(incl), heads(diff), spread(sq(INC[d]), GH), ALU.mult))
            dve.tensor_tensor(h[:, 4 * d + b, :], incl, bank[1][:], ALU.mult).then_inc(signal("intra"), 1)
            step(dve.tensor_tensor(heads(far), heads(diff), spread(sq(STR[d]), GH), ALU.mult))
            step(dve.tensor_tensor(far, far, bank[0][:], ALU.mult))
            step(dve.tensor_tensor(heads(far), heads(far), b4(beta), ALU.mult))
            step(dve.tensor_tensor(heads(near), heads(far), spread(sq("near"), GH), ALU.mult))
            step(dve.tensor_tensor(heads(far), heads(far), spread(sq("far"), GH), ALU.mult))
            dve.wait_ge(*seen("row_exp", n + 1))
            c = slice(b * P, (b + 1) * P)
            dve.tensor_tensor(A[:, 4 + 4 * d:8 + 4 * d, c], A[:, 12:16, c], heads(e_row), ALU.mult)\
                .then_inc(signal("masks_done"), 1)

        def gdn_masks_act(act, b, d):
            n = 2 * b + d
            act.wait_ge(*seen("g_rows", n + 1))
            if b:
                act.wait_ge(*seen("masks_done", n - 1))
            act.wait_ge(*seen("g_diff", n + 1))
            act.activation(W(20 + d), bank[2 + d][:], ACT.Exp).then_inc(signal("row_exp"), 1)
            act.activation(W(44 + d), W(44 + d), ACT.Exp).then_inc(signal("decay"), 1)

        def inverse_pe(pe, b, d, k):
            s = lambda i: scratch(d, i)
            p0, p1 = bank[4 + 2 * d][:], bank[5 + 2 * d][:]
            if b or INV_DVE[k - 1]:
                pe.wait_ge(*seen("inv_dve", inv_dve_at(b, d, k - 1)))
            if b or INV_ACT[k - 1]:
                pe.wait_ge(*seen("inv_act", inv_act_at(b, d, k - 1)))
            if k == 1:
                pe.wait_ge(*seen("masks_done", 2 * b + d + 1))
            work = {1: (("t", p0, S_NEAR, None),),
                    2: (("m", p0, S_NEAR_T, S_NEAR), ("m", p1, S_NEAR, S_NEAR_T)),
                    3: (("m", p0, S_2, S_B), ("m", p1, S_2T, S_2)),
                    4: (("m", p0, S_2, S_2T), ("m", p1, S_4, S_B)),
                    5: (("m", p0, S_4T, S_4),),
                    6: (("m", p0, S_NEAR, S_B),),
                    7: (("m", p0, S_FAR, S_B), ("t", p1, S_B, None)),
                    8: (("m", p0, S_2, S_4),),
                    9: (("m", p0, S_2, S_NEAR_T),),
                    10: (("m", p0, S_2, S_2T),)}[k]
            for what, dst, a, c in work:
                for j in range(GH):
                    if what == "t":
                        mm = pe.transpose(head(dst, j), head(s(a), j), sq("ident"))
                    else:
                        mm = pe.matmul(head(dst, j), head(s(a), j), head(s(c), j), start=True, stop=True)
            mm.then_inc(signal("inv_pe"), 1)

        def inverse_dve(dve, b, d, k, step):
            s = lambda i: scratch(d, i)
            p0, p1 = bank[4 + 2 * d][:], bank[5 + 2 * d][:]
            if k == 5:
                return
            dve.wait_ge(*seen("inv_pe", inv_pe_at(b, d, k)))
            if k == 1:
                step(dve.tensor_copy(s(S_NEAR_T), p0))
                ins = dve.tensor_tensor(heads(s(S_B)), spread(sq("ident"), GH), heads(p0), ALU.subtract)
            elif k == 2:
                ins = dve.tensor_copy(s(S_2), p0)
            elif k in (3, 4, 6):
                ins = dve.tensor_tensor(s(S_B), s(S_B), p1 if k == 4 else p0, ALU.add)
            elif k == 7:
                ins = dve.tensor_copy(s(S_4), p1)
            else:
                dst = {8: s(S_NEAR_T), 9: s(S_2T), 10: W(36 + 4 * d + b)}[k]
                ins = dve.tensor_tensor(dst, s(S_4), p0, ALU.subtract)
            ins.then_inc(signal("inv_dve"), 1)
            dve.wait_ge(*seen("inv_dve", inv_dve_at(b, d, k)))

        def inverse_act(act, b, d, k):
            s = lambda i: scratch(d, i)
            p0, p1 = bank[4 + 2 * d][:], bank[5 + 2 * d][:]
            got = {2: (S_2T, p1), 3: (S_4, p1), 4: (S_4T, p0), 5: (S_NEAR, p0), 7: (S_2, p0)}.get(k)
            if got:
                act.wait_ge(*seen("inv_pe", inv_pe_at(b, d, k)))
                act.activation(s(got[0]), got[1], ACT.Copy).then_inc(signal("inv_act"), 1)

        state = lambda d: W(44 + d)
        resid = lambda d: scratch(d, 0)
        v_new = lambda d: scratch(d, 1)
        v_dec = lambda d: scratch(d, 2)

        def chunk(d, i):
            n = i if d == 0 else GN - 1 - i
            return n, n // 2, 64 * (n % 2)

        def scan_init_dve(dve):
            dve.wait_ge(*seen("inv_dve", 2 * 9 * TT))
            for d in range(2):
                dve.memset(state(d), 0.0).then_inc(signal("scan_state"), 1)
                dve.memset(resid(d), 0.0).then_inc(signal("scan_zero"), 1)
                dve.memset(v_new(d), 0.0).then_inc(signal("scan_zero"), 1)
            dve.wait_ge(*seen("scan_zero", 4))

        def scan_pe(pe):
            pe.wait_ge(*seen("scan_zero", 4))
            for i in range(GN):
                for d in range(2):
                    n, b, r = chunk(d, i)
                    pe.wait_ge(*seen("scan_state", 2 * i + d + 1))
                    for j in range(GH):
                        mm = pe.matmul(bank[d][r:r + 64, j * P:(j + 1) * P], W(16 + j)[:, n * GC:(n + 1) * GC],
                                       head(state(d), j), start=True, stop=True)
                    mm.then_inc(signal("scan_ks"), 1)
                for d in range(2):
                    n, b, r = chunk(d, i)
                    pe.wait_ge(*seen("scan_resid", 2 * i + d + 1))
                    for j in range(GH):
                        mm = pe.matmul(bank[2 + d][r:r + 64, j * P:(j + 1) * P],
                                       W(36 + 4 * d + b)[:, j * P + r:j * P + r + 64], head(resid(d), j),
                                       start=True, stop=True)
                    mm.then_inc(signal("scan_y"), 1)
                for d in range(2):
                    n, b, r = chunk(d, i)
                    pe.wait_ge(*seen("scan_v", 2 * i + d + 1))
                    if i:
                        pe.wait_ge(*seen("scan_out", 2 * i - 1 + d))
                    for j in range(GH):
                        o = bank[4 + d][:, j * GC:(j + 1) * GC]
                        pe.matmul(o, head(state(d), j), W(4 + 4 * d + j)[:, n * GC:(n + 1) * GC],
                                  start=True, stop=False)
                        mm = pe.matmul(o, head(v_new(d), j), h[:, 4 * d + b, j * P + r:j * P + r + 64],
                                       start=False, stop=True)
                    mm.then_inc(signal("scan_o"), 1)
                    if i < GN - 1:
                        pe.wait_ge(*seen("scan_vdec", 2 * i + d + 1))
                        for j in range(GH):
                            mm = pe.matmul(head(bank[6 + d][:], j), W(28 + b)[r:r + 64, j * P:(j + 1) * P],
                                           v_dec(d)[r:r + 64, j * P:(j + 1) * P], start=True, stop=True)
                        mm.then_inc(signal("scan_kv"), 1)

        def scan_dve(dve):
            for i in range(GN):
                for d in range(2):
                    n, b, r = chunk(d, i)
                    dve.wait_ge(*seen("scan_ks", 2 * i + d + 1))
                    for j in range(GH):
                        c = slice(j * P, (j + 1) * P)
                        ins = dve.scalar_tensor_tensor(resid(d)[r:r + 64, c], bank[d][r:r + 64, c],
                                                       neg_eg[r:r + 64, b, 4 * d + j:4 * d + j + 1],
                                                       W(32 + b)[r:r + 64, c], ALU.mult, ALU.add)
                    ins.then_inc(signal("scan_resid"), 1)
                if i == GN - 1:
                    break
                for d in range(2):
                    n, b, r = chunk(d, i)
                    dve.wait_ge(*seen("scan_v", 2 * i + d + 1))
                    dve.tensor_tensor(heads(v_dec(d)[r:r + 64, :]), heads(bank[2 + d][r:r + 64, :]),
                                      spread(beta_rest[r:r + 64, b, 4 * d:4 * d + 4], P, at=2), ALU.mult)\
                        .then_inc(signal("scan_vdec"), 1)
                for d in range(2):
                    n, b, r = chunk(d, i)
                    dve.wait_ge(*seen("scan_kv", 2 * i + d + 1))
                    for j in range(GH):
                        c = slice(j * P, (j + 1) * P)
                        ins = dve.scalar_tensor_tensor(state(d)[:, c], state(d)[:, c],
                                                       eg_last[:, n, 4 * d + j:4 * d + j + 1], bank[6 + d][:, c],
                                                       ALU.mult, ALU.add)
                    ins.then_inc(signal("scan_state"), 1)

        def scan_act(act):
            for i in range(GN):
                for d in range(2):
                    n, b, r = chunk(d, i)
                    act.wait_ge(*seen("scan_y", 2 * i + d + 1))
                    if i:
                        act.wait_ge(*seen("scan_o", 2 * i - 1 + d))
                    for j in range(GH):
                        c = slice(j * P, (j + 1) * P)
                        ins = act.activation(v_new(d)[r:r + 64, c], bank[2 + d][r:r + 64, c], ACT.Copy,
                                             scale=beta[r:r + 64, b, 4 * d + j:4 * d + j + 1])
                    ins.then_inc(signal("scan_v"), 1)
                for d in range(2):
                    n, b, r = chunk(d, i)
                    act.wait_ge(*seen("scan_o", 2 * i + d + 1))
                    dst = A[:, (12, 20)[d]:(16, 24)[d], n * GC:(n + 1) * GC]
                    act.activation(dst, bank[4 + d][:, 0:GH * GC].rearrange("p (h n) -> p h n", h=GH),
                                   ACT.Copy).then_inc(signal("scan_out"), 1)

        def gdn_out_dve(dve):
            step = ordered(dve, "gdn_out_dve")
            dve.wait_ge(*seen("scan_out", 2 * GN))
            for j in range(GH):
                then(dve.tensor_tensor(W(12 + j), W(12 + j), W(20 + j), ALU.add), "gdn_sum")
            for j in range(GH):
                dve.wait_ge(*seen("gdn_std", j + 1))
                step(dve.reciprocal(W(20 + j), W(20 + j)))
                step(dve.scalar_tensor_tensor(W(12 + j), W(12 + j), col("gdn_norm_w"), W(20 + j), ALU.mult, ALU.mult))
                dve.tensor_tensor(W(12 + j), W(12 + j), W(24 + j), ALU.mult).then_inc(signal("y_gdn"), 1)

        def gdn_out_act(act):
            for j in range(GH):
                act.wait_ge(*seen("gdn_sum", j + 1))
                act.activation(W(16 + j), W(12 + j), ACT.Square).then_inc(signal("gdn_squared"), 1)
            for j in range(GH):
                act.wait_ge(*seen("gdn_summed", j + 1))
                act.activation(W(20 + j), bank[4 + j][:], ACT.Sqrt, bias=eps, scale=1.0 / GD)\
                    .then_inc(signal("gdn_std"), 1)

        def gdn_out_pe(pe):
            pe.wait_ge(*seen("scan_out", 2 * GN))
            for j in range(GH):
                pe.wait_ge(*seen("gdn_squared", j + 1))
                pe.matmul(bank[4 + j][:], sq("ones"), W(16 + j), start=True, stop=True).then_inc(signal("gdn_summed"), 1)

        MIXED = (0, 1, 2, 3, 12, 13, 14, 15)

        def out_pe(pe):
            pe.wait_ge(*seen("y_gdn", GH))
            pe.wait_ge(*seen("na_out", len(units)))
            project(pe, L["out"], lambda k: W(MIXED[k]))

        def add_gated(dve, gs, gate, n):
            for j, tile in enumerate(tiles_of(*gs)):
                b = read_tile(dve, tile, j == 0)
                dve.scalar_tensor_tensor(X(j), b[:], gate(j), X(j), ALU.mult, ALU.add)\
                    .then_inc(sem("tile_read"), 1)

        route_w = A[:, 32, 0:288].rearrange("p (k n) -> p k n", k=KD)
        grp8 = A[:, 33, 0:32]
        gmax8 = A[:, 33, 32:64]
        gidx8 = A[:, 33, 64:96].bitcast(U32)
        emax8 = A[:, 33, 96:128]
        eidx8 = A[:, 33, 128:160].bitcast(U32)
        gsel = A[:, 33, 160:176]
        gneg = A[:, 33, 176:192]
        gexp = A[:, 33, 192:208]
        gtop = A[:, 33, 208:212]
        gid = A[:, 33, 212:216]
        eid = A[:, 33, 216:224]
        r1 = A[:, 33, 224:228]
        r2 = A[:, 33, 228:232]
        gates = A[:, 33, 232:240]
        rank = A[:, 33, 240:248]
        quot = A[:, 33, 248:256]
        spill0 = A[:, 33, 256:264]
        over = A[:, 33, 264:272]
        blk = A[:, 33, 272:280]
        rem = A[:, 33, 280:288]
        pos = A[:, 33, 288:296]
        tok_id = A[:, 33, 296:300]
        n_spill = A[:, 33, 304:336]
        spill_end = A[:, 33, 336:368]
        spill_start = A[:, 33, 368:400]
        n_pairs = A[:, 33, 400:404]
        pos_u = A[:, 33, 408:416].bitcast(U32)
        pairs_i = A[0:1, 33, 416:417].bitcast(I32)
        logits = A[:, 34, 0:144]
        el = A[:, 34, 144:272]
        ohs = A[:, 34, 272:400]
        table_f = A[:, 34, 400:440]
        table_i = A[0:1, 34, 440:480].bitcast(I32)
        oh = A[:, 35, 0:256]
        prod = A[:, 35, 256:512]
        slot_tok = A[:, 36, 0:N_BLK].bitcast(U32)
        slot_cur = A[:, 36, 64:66].bitcast(U32)
        on_rem = lambda i: A[:, 38 + i // 4, (i % 4) * P:(i % 4 + 1) * P]
        on_blk = lambda i: A[:, 40, i * 64:i * 64 + N_BLK]

        def tokens_pe(pe):
            pe.wait_ge(*norm_at("n2", "out", KD))
            pe.wait_ge(sem("route_in"), 32)
            for t in range(TT):
                for c0, n, at in ((0, 4, 4 * t), (4, 32, 16 + 32 * t)):
                    for k in range(KD):
                        mm = pe.matmul(bank[5][:, at:at + n], Hn(k)[:, t * P:(t + 1) * P], route_w[:, k, c0:c0 + n],
                                       start=(k == 0), stop=(k == KD - 1))
            mm.then_inc(signal("logits"), 1)
            for i in range(2 * TT):
                if i >= 2:
                    pe.wait_ge(*seen("tok_copied", i - 1))
                for k in range(4):
                    kk = 4 * (i % 2) + k
                    mm = pe.transpose(bank[6 + i % 2][:, k * P:(k + 1) * P], Hn(kk)[:, (i // 2) * P:(i // 2 + 1) * P],
                                      sq("ident"))
                mm.then_inc(signal("tok_turned"), 1)
            pe.wait_ge(*seen("route_oh", 1))
            for t in range(TT):
                for u in range(t + 1):
                    pe.matmul(bank[4][:, t * 32:(t + 1) * 32], sq("before" if u == t else "ones"),
                              ohs[:, u * 32:(u + 1) * 32], start=(u == 0), stop=(u == t))
            for t in range(TT):
                mm = pe.matmul(bank[4][:, 128:160], sq("ones"), ohs[:, t * 32:(t + 1) * 32], start=(t == 0),
                               stop=(t == TT - 1))
            mm.then_inc(signal("route_cum"), 1)
            pe.wait_ge(*seen("route_place", 1))
            for i in range(2 * TT):
                mm = pe.matmul(bank[5][:, 0:N_BLK], on_rem(i), on_blk(i), start=(i == 0), stop=(i == 2 * TT - 1))
            mm.then_inc(signal("slot_tokens"), 1)

        def tokens_act(act):
            act.wait_ge(*seen("y_gdn", GH))
            rw = A[:, 32, 0:288].rearrange("p (k n) -> p k n", k=KD)
            act.wait_ge(*norm_at("n2", "std", 1))
            act.dma_start(rw[:, :, 0:4], w["router_group_w"].rearrange("(k p) n -> p k n", p=P))\
                .then_inc(sem("route_in"), 16)
            act.dma_start(rw[:, :, 4:36], w["router_expert_w"].rearrange("(k p) n -> p k n", p=P))\
                .then_inc(sem("route_in"), 16)

        def tokens_act2(act):
            for i in range(2 * TT):
                act.wait_ge(*seen("tok_turned", i + 1))
                act.activation(W(i), bank[6 + i % 2][:], ACT.Copy).then_inc(signal("tok_copied"), 1)
            act.wait_ge(*seen("tok_copied", 2 * TT))
            act.dma_start(tok_rows.rearrange("(t p) n -> p t n", p=P),
                          A[:, 0:8, :].rearrange("p (t a) n -> p t (a n)", t=TT)).then_inc(sem("tok_out"), 16)
            act.wait_ge(*seen("route_sub", 1))
            act.activation(gexp, gexp, ACT.Exp).then_inc(signal("route_exp"), 1)
            act.wait_ge(*seen("route_diff", 1))
            act.activation(r1, r1, ACT.Exp).then_inc(signal("route_exp"), 1)

        def route_dve(dve):
            step = ordered(dve, "route_dve")
            iota = square_iota
            dve.wait_ge(*seen("logits", 1))
            dve.memset(A[:, 28:30, :], 0.0).then_inc(signal("zero_rows"), 1)
            rg, re = row("router_group_b", 4), row("router_expert_b", 32)
            t4 = lambda ap: ap.rearrange("p (t n) -> p t n", t=TT)
            step(dve.tensor_tensor(t4(logits[:, 0:16]), t4(bank[5][:, 0:16]), spread(rg, TT), ALU.add))
            step(dve.tensor_tensor(t4(logits[:, 16:144]), t4(bank[5][:, 16:144]), spread(re, TT), ALU.add))
            step(dve.memset(grp8, -BIG))
            step(dve.tensor_copy(t4(grp8)[:, :, 0:4], t4(logits[:, 0:16])))
            for t in range(TT):
                s8 = slice(8 * t, 8 * t + 8)
                step(dve.max(gmax8[:, s8], grp8[:, s8]))
                step(dve.max_index(gidx8[:, s8], gmax8[:, s8], grp8[:, s8]))
            step(dve.tensor_copy(gid, t4(gidx8)[:, :, 0]))
            step(dve.tensor_tensor(t4(gsel), spread(iota[:, 0:4], TT), spread(gid, 4, at=2), ALU.is_equal))
            dve.tensor_tensor(t4(gexp), t4(logits[:, 0:16]), spread(t4(gmax8)[:, :, 0], 4, at=2),
                              ALU.subtract).then_inc(signal("route_sub"), 1)
            dve.wait_ge(*seen("route_exp", 1))
            step(dve.tensor_reduce(gtop, t4(gexp), AX_X, ALU.add))
            step(dve.reciprocal(gtop, gtop))
            step(dve.tensor_scalar(gneg, gsel, BIG, BIG, ALU.mult, ALU.subtract))
            g8 = lambda ap: ap.rearrange("p (g n) -> p g n", n=EPG)
            step(dve.tensor_tensor(g8(el), g8(logits[:, 16:144]), spread(gsel, EPG, at=2), ALU.mult))
            step(dve.tensor_tensor(g8(el), g8(el), spread(gneg, EPG, at=2), ALU.add))
            for t in range(TT):
                s8 = slice(8 * t, 8 * t + 8)
                step(dve.max(emax8[:, s8], el[:, 32 * t:32 * t + 32]))
                step(dve.max_index(eidx8[:, s8], emax8[:, s8], el[:, 32 * t:32 * t + 32]))
            step(dve.tensor_copy(eid.rearrange("p (t n) -> p t n", t=TT), t4(eidx8)[:, :, 0:2]))
            dve.tensor_tensor(r1, t4(emax8)[:, :, 1], t4(emax8)[:, :, 0], ALU.subtract).then_inc(signal("route_diff"), 1)
            e32 = lambda ap: ap.rearrange("p (s n) -> p s n", n=32)
            step(dve.tensor_tensor(e32(oh), spread(iota[:, 0:32], 8), spread(eid, 32, at=2), ALU.is_equal))
            ohk = oh.rearrange("p (t k n) -> p t k n", t=TT, k=2)
            dve.tensor_tensor(t4(ohs), ohk[:, :, 0, :], ohk[:, :, 1, :], ALU.add).then_inc(signal("route_oh"), 1)
            dve.wait_ge(*seen("route_exp", 2))
            step(dve.tensor_scalar(r2, r1, 1.0, None, ALU.add))
            step(dve.reciprocal(r2, r2))
            step(dve.tensor_tensor(gates[:, 0:4], r2, gtop, ALU.mult))
            step(dve.tensor_tensor(gates[:, 4:8], gates[:, 0:4], r1, ALU.mult))
            dve.wait_ge(*seen("route_cum", 1))
            pk = prod.rearrange("p (t k n) -> p t k n", t=TT, k=2)
            for k in range(2):
                step(dve.tensor_tensor(pk[:, :, k, :], ohk[:, :, k, :], t4(bank[4][:, 0:128]), ALU.mult))
            step(dve.tensor_reduce(rank, e32(prod), AX_X, ALU.add))
            cnt = bank[4][:, 128:160]
            step(dve.tensor_scalar(n_spill, cnt, float(P), None, ALU.is_gt))
            for j in range(2, TT):
                step(dve.scalar_tensor_tensor(n_spill, cnt, float(P * j), n_spill, ALU.is_gt, ALU.add))
            step(dve.tensor_tensor_scan(spill_end, sq("ones")[:, 0:32], n_spill, 0.0, ALU.mult, ALU.add))
            step(dve.tensor_tensor(spill_start, spill_end, n_spill, ALU.subtract))
            step(dve.tensor_tensor(e32(prod), e32(oh), spread(spill_start, 8), ALU.mult))
            step(dve.tensor_reduce(spill0, e32(prod), AX_X, ALU.add))
            step(dve.tensor_scalar(quot, rank, float(P), None, ALU.is_ge))
            step(dve.tensor_copy(over, quot))
            for j in range(2, TT):
                step(dve.scalar_tensor_tensor(quot, rank, float(P * j), quot, ALU.is_ge, ALU.add))
            step(dve.scalar_tensor_tensor(rem, quot, -float(P), rank, ALU.mult, ALU.add))
            step(dve.tensor_tensor(blk, spill0, quot, ALU.add))
            step(dve.tensor_tensor(blk, blk, eid, ALU.subtract))
            step(dve.scalar_tensor_tensor(blk, blk, float(N_EXP - 1), over, ALU.add, ALU.mult))
            step(dve.tensor_tensor(blk, blk, eid, ALU.add))
            step(dve.scalar_tensor_tensor(pos, blk, float(P), rem, ALU.mult, ALU.add))
            step(dve.tensor_copy(pos_u, pos))
            for t in range(TT):
                step(dve.tensor_scalar(tok_id[:, t:t + 1], part_id[:, 0:1], float(P * t), None, ALU.add))
            for i in range(2 * TT):
                dve.tensor_scalar(on_rem(i), iota, rem[:, i:i + 1], None, ALU.is_equal)
                ins = dve.tensor_scalar(on_blk(i), iota[:, 0:N_BLK], blk[:, i:i + 1], tok_id[:, i // 2:i // 2 + 1],
                                        ALU.is_equal, ALU.mult)
            ins.then_inc(signal("route_place"), 1)
            step(dve.tensor_copy(table_f[:, 0:32], iota[:, 0:32]))
            step(dve.tensor_tensor(e32(prod), spread(iota[:, 0:8], 32, at=2), spread(spill_end, 8), ALU.is_ge))
            step(dve.tensor_reduce(table_f[:, 32:40], e32(prod), AX_X, ALU.add))
            step(dve.tensor_scalar(table_f, table_f, float(N_EXP - 1), None, ALU.min))
            step(dve.tensor_copy(table_i, table_f[0:1, :]))
            step(dve.tensor_scalar(n_pairs, iota[:, 0:4], 2.0, None, ALU.mult))
            step(dve.tensor_scalar(n_pairs, n_pairs, spill_end[:, 31:32], None, ALU.is_lt))
            step(dve.tensor_reduce(rank[:, 0:1], n_pairs, AX_X, ALU.add))
            step(dve.tensor_scalar(pairs_i, rank[0:1, 0:1], float(N_EXP // 2), None, ALU.add))
            dve.wait_ge(*seen("slot_tokens", 1))
            dve.tensor_copy(slot_tok, bank[5][:, 0:N_BLK]).then_inc(signal("route_done"), 1)
            dve.wait_ge(*seen("route_done", 1))

        moe_w = lambda s, i: (ring[:, i, :] if s == 0 and i < 3 else
                              ring[:, 3, :] if i == 0 else
                              A[:, 8 * (i - 1):8 * i, :].rearrange("p a n -> p (a n)"))
        rows_in = lambda s: A[:, 16 + 2 * s:18 + 2 * s, :].rearrange("p a n -> p (a n)")
        rows_t = lambda s: A[:, 20 + 2 * s:22 + 2 * s, :].rearrange("p a n -> p (a n)")
        hid = lambda s: W(24 + s)
        gate_act = lambda s: W(26 + s)
        rows_out = lambda s: A[:, 28 + 2 * s:30 + 2 * s, :].rearrange("p a n -> p (a n)")

        def pairs(eng):
            eng.wait_ge(*seen("route_done", 1))
            return eng.value_load(pairs_i, min_val=N_EXP // 2, max_val=N_BLK // 2)

        def moe_sync(sp):
            mats = [w[f"expert_w{i}"].rearrange(f"e (p k) n -> e p (k n)", p=P) for i in (1, 3, 2)]
            sp.wait_ge(*seen("zero_rows", 1))
            for b in range(N_EXP, N_BLK):
                sp.dma_start(slot_rows[b * P:(b + 1) * P, :], A[:, 28:30, :].rearrange("p a n -> p (a n)"))\
                    .then_inc(sem("spill_zeroed"), 16)
            n = pairs(sp)
            sp.wait_ge(sem("tok_out"), 16)
            with sp.Fori(0, n) as i:
                for s in range(2):
                    e = sp.value_load(table_i[:, bass.ds(2 * i + s, 1)], min_val=0, max_val=N_EXP - 1)
                    for j in range(3):
                        sp.wait_ge(sem(f"moe_{('gated', 'upped', 'downed')[j]}"), 2 * i + s + 1)
                        sp.dma_start(moe_w(s, j), mats[j][bass.ds(e, 1), :, :].rearrange("e p n -> (e p) n"))\
                            .then_inc(sem(f"moe_w{j}{s}"), 16)

        def moe_pool(pool):
            n = pairs(pool)
            pool.wait_ge(sem("tok_out"), 16)
            with pool.Fori(0, n) as i:
                for s in range(2):
                    pool.wait_ge(sem("moe_rows_free"), 2 * i + s + 1)
                    pool.tensor_copy(slot_cur[:, s:s + 1], slot_tok[:, bass.ds(2 * i + s, 1)])\
                        .then_inc(sem("moe_idx"), 1)
                    pool.wait_ge(sem("moe_idx"), 2 * i + s + 1)
                    pool.sem_inc(sem("moe_gathers"), 1)
                    pool.indirect_dma_start(rows_in(s), None, tok_rows,
                                            bass.IndirectOffsetOnAxis(ap=slot_cur[:, s:s + 1], axis=0))\
                        .then_inc(sem(f"moe_rows{s}"), 16)

        def moe_pe(pe):
            n = pairs(pe)
            pe.wait_ge(*seen("slot_tokens", 1))
            for name in ("gated", "upped", "downed", "rows_free"):
                pe.sem_inc(sem(f"moe_{name}"), 2)
            with pe.Fori(0, n) as i:
                for s in range(2):
                    pe.wait_ge(sem(f"moe_rows{s}"), 16 * i + 16)
                    pe.wait_ge(sem("moe_y_read"), 2 * i + s + 1)
                    for k in range(KD):
                        mm = pe.transpose(bank[2 * s + k // 4][:, (k % 4) * P:(k % 4 + 1) * P],
                                          rows_in(s)[:, k:D:KD], sq("ident"))
                    mm.then_inc(sem("moe_rows_free"), 1)
                for s in range(2):
                    pe.wait_ge(sem("moe_rows_t"), 2 * i + s + 1)
                    pe.wait_ge(sem("moe_hid"), 2 * i + s + 1)
                    for j in range(2):
                        pe.wait_ge(sem(f"moe_w{j}{s}"), 16 * i + 16)
                        wt = moe_w(s, j).rearrange("p (k n) -> p k n", k=KD)
                        for f in range(4):
                            for k in range(KD):
                                mm = pe.matmul(bank[4 + 2 * s + j][:, f * P:(f + 1) * P], wt[:, k, f:D_EXP:4],
                                               rows_t(s)[:, k * P:(k + 1) * P], start=(k == 0), stop=(k == KD - 1))
                        mm.then_inc(sem(f"moe_{('gated', 'upped')[j]}"), 1)
                for s in range(2):
                    pe.wait_ge(sem("moe_hid"), 2 * i + s + 3)
                    pe.wait_ge(sem(f"moe_w2{s}"), 16 * i + 16)
                    wt = moe_w(s, 2).rearrange("p (f n) -> p f n", f=4)
                    for c in range(2):
                        for f in range(4):
                            mm = pe.matmul(bank[2 * s + c][:], hid(s)[:, f * P:(f + 1) * P],
                                           wt[:, f, c * 512:(c + 1) * 512], start=(f == 0), stop=(f == 3))
                    mm.then_inc(sem("moe_downed"), 1)

        def moe_dve(dve):
            n = pairs(dve)
            dve.sem_inc(sem("moe_hid"), 2)
            with dve.Fori(0, n) as i:
                for s in range(2):
                    dve.wait_ge(sem("moe_rows_free"), 2 * i + s + 3)
                    for c in range(2):
                        ins = dve.tensor_copy(rows_t(s)[:, c * 512:(c + 1) * 512], bank[2 * s + c][:])
                    ins.then_inc(sem("moe_rows_t"), 1)
                for s in range(2):
                    dve.wait_ge(sem("moe_silu"), 2 * i + s + 1)
                    dve.wait_ge(sem("moe_upped"), 2 * i + s + 3)
                    dve.tensor_tensor(hid(s), gate_act(s), bank[5 + 2 * s][:], ALU.mult)\
                        .then_inc(sem("moe_hid"), 1)

        def moe_act(act):
            n = pairs(act)
            act.sem_inc(sem("moe_y_read"), 2)
            act.wait_ge(sem("spill_zeroed"), 16 * (N_BLK - N_EXP))
            out_v = slot_rows.rearrange("(b p) n -> b p n", p=P)
            with act.Fori(0, n) as i:
                for s in range(2):
                    act.wait_ge(sem("moe_gated"), 2 * i + s + 3)
                    act.activation(gate_act(s), bank[4 + 2 * s][:], ACT.Silu).then_inc(sem("moe_silu"), 1)
                for s in range(2):
                    act.wait_ge(sem("moe_downed"), 2 * i + s + 3)
                    for c in range(2):
                        ins = act.activation(rows_out(s)[:, c * 512:(c + 1) * 512], bank[2 * s + c][:], ACT.Copy)
                    ins.then_inc(sem("moe_y_read"), 1)
                    act.wait_ge(sem("moe_y_read"), 2 * i + s + 3)
                    act.dma_start(out_v[bass.ds(2 * i + s, 1), :, :].rearrange("b p n -> (b p) n"), rows_out(s))\
                        .then_inc(sem(f"moe_out{s}"), 16)
                for s in range(2):
                    act.wait_ge(sem(f"moe_out{s}"), 16 * i + 16)
            act.sem_inc(sem("moe_written"), 1)

        def combine_pool(pool):
            pool.wait_ge(sem("moe_written"), 1)
            for t in range(TT):
                for k in range(2):
                    i = 2 * t + k
                    pool.indirect_dma_start(A[:, 2 * i:2 * i + 2, :].rearrange("p a n -> p (a n)"), None, slot_rows,
                                            bass.IndirectOffsetOnAxis(ap=pos_u[:, i:i + 1], axis=0))\
                        .then_inc(sem(f"rows_back{t}"), 16)

        def combine_dve(dve):
            for t in range(TT):
                dve.wait_ge(sem(f"rows_back{t}"), 32)
                a0 = A[:, 4 * t:4 * t + 2, :].rearrange("p a n -> p (a n)")
                a1 = A[:, 4 * t + 2:4 * t + 4, :].rearrange("p a n -> p (a n)")
                dve.tensor_scalar(a0, a0, gates[:, t:t + 1], None, ALU.mult).then_inc(signal("comb_dve"), 1)
                dve.wait_ge(*seen("comb_dve", t + 1))
                dve.scalar_tensor_tensor(a0, a1, gates[:, 4 + t:5 + t], a0, ALU.mult, ALU.add)\
                    .then_inc(signal("combined"), 1)
            for k in range(KD):
                dve.wait_ge(*seen("comb_turned", k + 1))
                dve.scalar_tensor_tensor(X(k), bank[4 + k % 2][:], mod[:, 40 + k:41 + k], X(k), ALU.mult, ALU.add)\
                    .then_inc(signal("x_moe"), 1)

        def combine_pe(pe):
            pe.wait_ge(*seen("combined", TT))
            for k in range(KD):
                if k >= 2:
                    pe.wait_ge(*seen("x_moe", k - 1))
                for t in range(TT):
                    a0 = A[:, 4 * t:4 * t + 2, :].rearrange("p a n -> p (a n)")
                    mm = pe.transpose(bank[4 + k % 2][:, t * P:(t + 1) * P], a0[:, k * P:(k + 1) * P], sq("ident"))
                mm.then_inc(signal("comb_turned"), 1)

        square_iota = square[:, SQ["iota"], :]
        part_id = square[:, SQ["part"], :]
        TMP = lambda i: W(44 + i)
        n1_sq, n1_r = (lambda i: W(12 + i)), W(14)

        def block1_sync(sp):
            sp.dma_start(A[:, 0:8, :].rearrange("p (t a) n -> p t (a n)", t=TT),
                         w["x"].rearrange("b (t p) n -> p (b t) n", p=P)).then_inc(sem("x_in"), 16)
            load_weights(sp, order[:L["out"][-1].index + 1])
            moe_sync(sp)

        def load_weights(sp, gs):
            for g in gs:
                if g.index >= RING:
                    name, v = order[g.index - RING].release
                    sp.wait_ge(sem(name), v)
                sp.dma_start(ring_tile(g), g.src).then_inc(sem(f"ring_loaded{g.slot}"), 16)

        def block1_pe(pe):
            setup_pe(pe)
            ada_pe(pe, L["ada"], small[:, 4:12], "cond")
            norm_pe(pe, "n1", X, n1_sq)
            in_pe(pe)
            na_pe(pe)
            gdn_norm_pe(pe)
            gdn_gates_pe(pe)
            gdn_turn_pe(pe)
            for b in range(TT):
                gdn_masks_pe(pe, b)
                for k in range(1, 11):
                    for d in range(2):
                        inverse_pe(pe, b, d, k)
            scan_pe(pe)
            gdn_out_pe(pe)
            out_pe(pe)
            norm_pe(pe, "n2", X, TMP)
            tokens_pe(pe)
            moe_pe(pe)
            combine_pe(pe)
            norm_pe(pe, "n3", X, TMP)

        def block1_act(act):
            setup_act(act)
            for g in L["ada"]:
                ada_act(act, g)
            bias_act(act)
            norm_act(act, "n1", X, n1_sq, n1_r, eps, shift=lambda k: mod[:, k:k + 1], dst=Hn,
                     ready=(seen("x_ready", 2 * KD),))
            in_act(act)
            na_act(act)
            gdn_norm_act(act)
            gdn_gates_act(act)
            gdn_turn_act(act)
            for b in range(TT):
                for d in range(2):
                    gdn_masks_act(act, b, d)
                for k in range(1, 11):
                    for d in range(2):
                        inverse_act(act, b, d, k)
            scan_act(act)
            gdn_out_act(act)
            norm_act(act, "n2", X, TMP, W(46), eps, shift=lambda k: mod[:, 24 + k:25 + k], dst=Hn,
                     ready=((sem("tile_read"), L["out"][-1].first_tile + 4),))
            tokens_act(act)
            tokens_act2(act)
            moe_act(act)
            norm_act(act, "n3", X, TMP, W(46), eps, ready=(seen("x_moe", KD),))

        def block1_dve(dve):
            setup_dve(dve)
            ada_dve(dve, L["ada"][-1], 0, 16, col("b_ada", 0, 48), ((0, col("norm_mix_w", 0, 8)),), "ada_ready")
            norm_dve(dve, "n1", X, n1_r, lambda k: mod[:, 8 + k:9 + k], Hn)
            in_dve(dve)
            bias_dve(dve)
            na_dve(dve)
            gdn_norm_dve(dve)
            gdn_gates_dve(dve)
            step = ordered(dve, "masks_dve")
            for b in range(TT):
                for d in range(2):
                    gdn_masks_dve(dve, b, d, step)
                for k in range(1, 11):
                    for d in range(2):
                        inverse_dve(dve, b, d, k, step)
            scan_init_dve(dve)
            scan_dve(dve)
            gdn_out_dve(dve)
            add_gated(dve, L["out"], lambda j: mod[:, 16 + j:17 + j], "out")
            norm_dve(dve, "n2", X, W(46), lambda k: mod[:, 32 + k:33 + k], Hn)
            route_dve(dve)
            moe_dve(dve)
            combine_dve(dve)
            norm_dve(dve, "n3", X, W(46), lambda k: col("final_norm_w", k), X)

        def block1_pool(pool):
            sum_pool(pool, [L[f"ada{i}"][0] for i in range(4, 12)], small[:, 4:12], "cond")
            moe_pool(pool)
            combine_pool(pool)

        row2 = lambda i: A[:, 32 + 2 * i:34 + 2 * i, :].rearrange("p a n -> p (a n)")
        ROW2_V = ("gm_norm_g_2", "gm_norm_b_2", "gm_b_s_2", "b_v")
        v_tok = lambda t: A[:, 2 * t:2 * t + 2, :].rearrange("p a n -> p (a n)")
        i_tok = lambda t: A[:, 32 + 2 * t:34 + 2 * t, :].rearrange("p a n -> p (a n)")
        bias_i = A[:, 40:42, :].rearrange("p a n -> p (a n)")
        stats = small[:, 16:64].rearrange("p (t a n) -> p t a n", t=TT, a=2)
        moments = small[:, 64:72].rearrange("p (t n) -> p t n", t=TT)
        v_rstd = small[:, 72:76]
        lb = small[:, 96:104]
        one_less_lb = small[:, 104:112]
        neg_bf = small[:, 112:120]
        decays = small[:, 120:152]
        spatial = lambda g: h[:, g // 4, (g % 4) * P:(g % 4 + 1) * P]
        spatial_raw = lambda g: h[:, 2 + g // 4, (g % 4) * P:(g % 4 + 1) * P]
        keep16 = W(47)

        def row_of(name, n, at=0):
            src = w["rows2"]
            return bass.AP(tensor=src.tensor, offset=src.offset + ROW2[name] + at, ap=[[0, P], [1, n]])

        def block2_loads(act):
            act.wait_ge(*norm_at("n3", "squared", 1))
            for i, (name, at) in enumerate((("gm_norm_g_2", 0), ("gm_norm_b_2", 0), ("gm_b_s_2", 0),
                                            ("b_in_2", 1024))):
                act.dma_start(row2(i), row_of(name, 1024, at)).then_inc(sem("rows2_in"), 16)
            act.dma_start(keep16, w["tables"][2]).then_inc(sem("rows2_in"), 16)
            act.dma_start(bias_i, row_of("b_in_2", 1024, 4096)).then_inc(sem("rows2_in"), 16)
            act.dma_start(h[:, 2:4, :].rearrange("p a (g n) -> p (a g) n", g=4),
                          w["gm_w_s_2"].rearrange("g p n -> p g n")).then_inc(sem("spatial_in"), 16)

        def spatial_pe(pe):
            pe.wait_ge(sem("spatial_in"), 16)
            for i in range(2):
                for g in range(4):
                    mm = pe.transpose(bank[6 + i][:, g * P:(g + 1) * P], spatial_raw(4 * i + g), sq("ident"))
                mm.then_inc(signal("spatial_turned"), 1)

        def spatial_dve(dve):
            for i in range(2):
                dve.wait_ge(*seen("spatial_turned", i + 1))
                dve.tensor_copy(h[:, i, :], bank[6 + i][:]).then_inc(signal("spatial"), 1)
            dve.wait_ge(*seen("spatial", 2))
            for i in range(2):
                dve.memset(h[64:128, i, :].rearrange("p (g n) -> p g n", g=4)[:, :, 0:64], 0.0)\
                    .then_inc(signal("spatial"), 1)

        v_slices, u_slices, ga_slices = deep_slices(*L["v2"]), tile_slices(*L["u2"]), tile_slices(*L["ga2"])
        gm_slices = v_slices + u_slices + ga_slices
        for i, s in enumerate(gm_slices):
            s.before = gm_slices[i - 2] if i >= 2 else None
        gm_high = lambda slot: h[:, 4 + 2 * slot:6 + 2 * slot, :].rearrange("p a n -> p (a n)")
        x0_high, x0_low = (lambda k: W(16 + k)), (lambda k: W(24 + k))

        fq_slices, i_slices = tile_slices(*L["f2"], *L["q2"]), deep_slices(*L["i2"])
        fqi_slices = fq_slices + i_slices
        for i, s in enumerate(fqi_slices):
            s.before = fqi_slices[i - 2] if i >= 2 else None
        fqi_high = lambda slot: A[:, 44 - 2 * slot:46 - 2 * slot, :].rearrange("p a n -> p (a n)")
        assert fqi_slices[0].q % 2 == 0

        def gmlp_pe(pe):
            project_tokens_split(pe, v_slices, gm_high, x0_high, x0_low,
                                 lambda k: pe.wait_ge(*seen("x0_split", k + 1)))
            project_split(pe, u_slices, gm_high, x0_high, x0_low)
            pe.wait_ge(*seen("v_normed", TT))
            pe.wait_ge(*seen("spatial", 4))
            for g in range(KD):
                if g >= 2:
                    pe.wait_ge(*seen("spatial_added", g - 1))
                for t in range(TT):
                    mm = pe.matmul(bank[4 + g % 2][:, t * P:(t + 1) * P], v_tok(t)[:, g * P:(g + 1) * P], spatial(g),
                                   start=True, stop=True)
                mm.then_inc(signal("spatial_mixed"), 1)
            pe.wait_ge(*seen("y_a", KD))
            project(pe, L["wa2"], lambda k: W(8 + k))
            project_split(pe, ga_slices, gm_high, x0_high, x0_low)

        def gmlp_dve(dve):
            step = ordered(dve, "gmlp_dve")
            dve.wait_ge(sem("rows2_in"), 16 * 6)
            for s in gm_slices[:2]:
                split_low(dve, s, gm_high)
            for k in range(KD):
                dve.wait_ge(*norm_at("ln0", "out", k + 1))
                step(dve.tensor_copy(parts(x0_high(k)), X(k)))
                dve.tensor_tensor(parts(x0_low(k)), X(k), parts(x0_high(k)), ALU.subtract)\
                    .then_inc(signal("x0_split"), 1)
            for j, g in enumerate(L["v2"]):
                for s in gm_slices[4 * j + 2:4 * j + 6]:
                    split_low(dve, s, gm_high)
                for t in range(TT):
                    b = read_tile(dve, g.first_tile + t, j == t == 0)
                    c = slice(512 * j, 512 * j + 512)
                    dve.tensor_tensor(v_tok(t)[:, c], b[:], row2(3)[:, c], ALU.add).then_inc(sem("tile_read"), 1)

            def v_stats(t):
                for j in range(2):
                    dve.wait_ge(*seen("v_gelu", 4 * j + t + 1))
                    step(dve.bn_stats(stats[:, t, j, :], v_tok(t)[:, 512 * j:512 * j + 512]))
                dve.bn_aggr(moments[:, t, :], stats[:, t, :, :]).then_inc(signal("v_moments"), 1)

            def v_norm(t):
                v = v_tok(t)
                step(dve.tensor_scalar(v, v, moments[:, t, 0:1], v_rstd[:, t:t + 1], ALU.subtract, ALU.mult))
                step(dve.tensor_tensor(v, v, row2(0), ALU.mult))
                dve.tensor_tensor(v, v, row2(1), ALU.add).then_inc(signal("v_normed"), 1)

            for j in range(KD):
                split_low(dve, gm_slices[10 + j], gm_high)
                if j < TT:
                    v_stats(j)
                if j == TT + 1:
                    dve.wait_ge(*seen("v_std", 1))
                    step(dve.reciprocal(v_rstd, v_rstd))
                if j > TT:
                    v_norm(j - TT - 1)
            v_norm(TT - 1)
            dve.wait_ge(sem("tile_read"), L["u2"][-1].first_tile + 4)
            for g in range(KD):
                dve.wait_ge(*seen("spatial_mixed", g + 1))
                t4 = W(42 + g % 2)
                then(dve.tensor_tensor(heads(t4), heads(bank[4 + g % 2][:]), spread(head(row2(2), g), TT), ALU.add),
                     "spatial_added")
                dve.wait_ge(*seen("spatial_added", g + 1))
                dve.tensor_tensor(W(8 + g), W(8 + g), t4, ALU.mult).then_inc(signal("y_a"), 1)
            for j, tile in enumerate(tiles_of(*L["ga2"])):
                if 18 + j < len(gm_slices):
                    split_low(dve, gm_slices[18 + j], gm_high)
                dve.wait_ge(sem("tile_read"), tile + 1)
                dve.tensor_tensor(W(j), W(j), W(42 + j % 2), ALU.mult).then_inc(signal("branch_a"), 1)
                dve.tensor_copy(parts(X(j)), parts(x0_high(j)))
                if j == 6:
                    split_low(dve, fqi_slices[0], fqi_high)
            dve.wait_ge(sem("tile_ready"), L["ga2"][-1].first_tile + 4)
            for k in range(KD):
                dve.tensor_copy(parts(Hn(k)), parts(x0_low(k))).then_inc(signal("x0_moved"), 1)
            split_low(dve, fqi_slices[1], fqi_high)

        def gmlp_act(act):
            for s in gm_slices[:2]:
                split_high(act, s, gm_high)
            for j, g in enumerate(L["v2"]):
                for s in gm_slices[4 * j + 2:4 * j + 6]:
                    split_high(act, s, gm_high)
                for t in range(TT):
                    act.wait_ge(sem("tile_read"), g.first_tile + t + 1)
                    v = v_tok(t)[:, 512 * j:512 * j + 512]
                    act.activation(v, v, ACT.Gelu_apprx_tanh).then_inc(signal("v_gelu"), 1)
            for j, tile in enumerate(tiles_of(*L["u2"])):
                split_high(act, gm_slices[10 + j], gm_high)
                b = read_tile(act, tile, j == 0)
                act.activation(W(8 + j), b[:], ACT.Gelu_apprx_tanh, bias=col("b_in_2", j)).then_inc(sem("tile_read"), 1)
                if j == TT:
                    act.wait_ge(*seen("v_moments", TT))
                    act.activation(v_rstd, moments[:, :, 1], ACT.Sqrt, bias=ln_eps).then_inc(signal("v_std"), 1)
            for j, tile in enumerate(tiles_of(*L["wa2"])):
                b = read_tile(act, tile)
                act.activation(W(j), b[:], ACT.Copy).then_inc(sem("tile_read"), 1)
            for j, tile in enumerate(tiles_of(*L["ga2"])):
                if 18 + j < len(gm_slices):
                    split_high(act, gm_slices[18 + j], gm_high)
                b = read_tile(act, tile)
                if j >= 2:
                    act.wait_ge(*seen("branch_a", j - 1))
                act.activation(W(42 + j % 2), b[:], ACT.Sigmoid, bias=col("b_in_2", 48 + j))\
                    .then_inc(sem("tile_read"), 1)
                if j == 6:
                    split_high(act, fqi_slices[0], fqi_high)
            act.wait_ge(*seen("branch_a", KD))
            split_high(act, fqi_slices[1], fqi_high)

        SPANS = (32, 64, 128)
        hg_b16, hg_b128, hg_e, hg_qe, hg_ke, hg_sum, hg_e2 = (W(i) for i in range(40, 47))
        i_head = lambda b, j: i_tok(b)[:, j * P:(j + 1) * P]

        def lb_dve(dve):
            dve.tensor_tensor(small[:, 152:160], col("hg_lb_logits_2", 0, 8), col("hg_lb_logits_2", 8, 8),
                              ALU.subtract).then_inc(signal("lb_diff"), 1)
            dve.tensor_scalar(neg_bf, col("b_in_2", 24, 8), -1.0, None, ALU.mult).then_inc(signal("lb_diff"), 1)

        def lb_act(act):
            act.wait_ge(*seen("lb_diff", 2))
            act.activation(lb, small[:, 152:160], ACT.Sigmoid).then_inc(signal("lb"), 1)
            act.activation(one_less_lb, small[:, 152:160], ACT.Sigmoid, scale=-1.0).then_inc(signal("lb"), 1)
            act.wait_ge(*seen("lb", 2))

        def hg_in_act(act):
            def log_f(j):
                act.wait_ge(*seen("hg_f", j + 1))
                act.activation(W(16 + j), W(16 + j), ACT.Ln).then_inc(signal("hg_logf"), 1)

            for j, tile in enumerate(tiles_of(*L["f2"])):
                split_high(act, fqi_slices[j + 2], fqi_high)
                b = read_tile(act, tile)
                act.activation(W(8 + j), b[:], ACT.Sigmoid, bias=neg_bf[:, j:j + 1], scale=-1.0)
                act.activation(W(16 + j), b[:], ACT.Sigmoid, bias=col("b_in_2", 24 + j)).then_inc(sem("tile_read"), 1)
                if j:
                    log_f(j - 1)
            log_f(KD - 1)
            for j, tile in enumerate(tiles_of(*L["q2"])):
                split_high(act, fqi_slices[10 + j], fqi_high)
                b = read_tile(act, tile)
                act.activation(W(24 + j), b[:], ACT.Silu, bias=col("b_in_2", 16 + j)).then_inc(sem("tile_read"), 1)
            for s in fqi_slices[18:]:
                split_high(act, s, fqi_high)

        def hg_in_dve(dve):
            dve.wait_ge(*seen("lb", 2))
            for j, tile in enumerate(tiles_of(*L["f2"])):
                split_low(dve, fqi_slices[j + 2], fqi_high)
                dve.wait_ge(sem("tile_read"), tile + 1)
                dve.tensor_scalar(W(16 + j), W(16 + j), one_less_lb[:, j:j + 1], lb[:, j:j + 1], ALU.mult, ALU.add)\
                    .then_inc(signal("hg_f"), 1)
                dve.tensor_scalar(W(8 + j), W(8 + j), one_less_lb[:, j:j + 1], None, ALU.mult).then_inc(signal("hg_k"), 1)
            for s in fqi_slices[10:18]:
                split_low(dve, s, fqi_high)
            for j, g in enumerate(L["i2"]):
                for s in fqi_slices[4 * j + 18:4 * j + 22]:
                    split_low(dve, s, fqi_high)
                for t in range(TT):
                    b = read_tile(dve, g.first_tile + t, j == t == 0)
                    c = slice(512 * j, 512 * j + 512)
                    dve.tensor_tensor(i_tok(t)[:, c], b[:], bias_i[:, c], ALU.add).then_inc(sem("tile_read"), 1)
            dve.wait_ge(sem("tile_ready"), L["i2"][-1].first_tile + 4)
            for k in range(KD):
                dve.tensor_tensor(X(k), parts(X(k)), parts(Hn(k)), ALU.add).then_inc(signal("x0_whole"), 1)
            dve.wait_ge(*seen("hg_k", KD))
            dve.wait_ge(sem("tile_read"), L["i2"][-1].first_tile + 4)

        def in_pairs(pe, g, m, rhs, between):
            tile = g.first_tile + m
            weights_here(pe, g)
            bank_free(pe, tile)
            for i in range(4):
                for k in (2 * i, 2 * i + 1):
                    mm = pe.matmul(bank[tile % 4][:], ring_tile(g)[:, k, m * P:(m + 1) * P], rhs(k),
                                   start=(k == 0), stop=(k == KD - 1))
                if i == 3:
                    mm.then_inc(sem("tile_ready"), 1)
                between(i)

        def hg_pe(pe):
            project_split(pe, fq_slices, fqi_high, X, Hn, first=lambda k: pe.wait_ge(*seen("x0_moved", k + 1)))
            project_tokens_split(pe, i_slices, fqi_high, X, Hn, lambda k: None)
            pe.wait_ge(*seen("x0_whole", KD))

            def level(j, i):
                pe.wait_ge(*seen("hg_qk", 4 * j + i + 1))
                for b in range(TT):
                    c = slice(b * P, (b + 1) * P)
                    mm = pe.matmul(bank[4 + i % 2][:, c], hg_ke[:, c], hg_qe[:, c], start=True, stop=True)
                mm.then_inc(signal("hg_scored"), 1)

            def turn(j):
                pe.wait_ge(*seen("hg_kend", j + 1))
                for b in range(TT):
                    mm = pe.transpose(head(bank[6][:], b), head(W(8 + j), b), sq("ident"))
                mm.then_inc(signal("hg_turned"), 1)

            def kv(j):
                pe.wait_ge(*seen("hg_ktok", j + 1))
                for b in range(TT - 1):
                    mm = pe.matmul(head(bank[7][:], b), head(W(16 + j), b), i_head(b, j), start=True, stop=True)
                mm.then_inc(signal("hg_kv"), 1)

            def outs(j):
                pe.wait_ge(*seen("hg_state", j + 1))
                for b in range(TT):
                    mm = pe.matmul(head(bank[5][:], b), i_head(b, j), head(hg_sum, b), start=True, stop=(b == 0))
                    if b:
                        mm = pe.matmul(head(bank[5][:], b), head(W(8 + j), b - 1), head(W(24 + j), b),
                                       start=False, stop=True)
                mm.then_inc(signal("hg_o"), 1)

            def during(j):
                def between(i):
                    if i == 0 and j:
                        turn(j - 1)
                    if i == 1:
                        if j:
                            kv(j - 1)
                        if j < HH:
                            level(j, 0)
                    if i == 2:
                        if j:
                            outs(j - 1)
                            pe.wait_ge(*seen("hg_out", j))
                        if j < HH:
                            level(j, 1)
                    if i == 3 and j < HH:
                        level(j, 2)
                        level(j, 3)
                return between

            tiles = [(g, m) for g in L["g2"] + L["gb2"] for m in range(4)]
            for j in range(HH + 1):
                in_pairs(pe, *tiles[j], X, during(j))
            for j in range(HH):
                if HH + 1 + j < 2 * HH:
                    in_pairs(pe, *tiles[HH + 1 + j], X, lambda i: None)
                pe.wait_ge(*seen("hg_squared", j + 1))
                pe.matmul(bank[4 + j % 2][:], sq("ones"), W(42 + 2 * (j % 2)), start=True, stop=True)\
                    .then_inc(signal("hg_summed"), 1)
            pe.wait_ge(*seen("y_b", HH))
            project(pe, L["wb2"], lambda k: W(24 + k))
            pe.wait_ge(*seen("merged", KD))
            project(pe, L["wo2"], W)

        def hg_dve(dve):
            step = ordered(dve, "hg_dve")
            n = [0]

            def exps(k):
                n[0] += k
                dve.wait_ge(*seen("hg_exp", n[0]))

            def states(j):
                s = lambda b: head(W(8 + j), b)
                dve.wait_ge(*seen("hg_kv", j + 1))
                step(dve.tensor_copy(s(0), bank[7][:, 0:P]))
                step(dve.scalar_tensor_tensor(s(1), s(0), decays[:, 4 * j + 1:4 * j + 2], bank[7][:, P:2 * P],
                                              ALU.mult, ALU.add))
                dve.scalar_tensor_tensor(s(2), s(1), decays[:, 4 * j + 2:4 * j + 3], bank[7][:, 2 * P:3 * P],
                                         ALU.mult, ALU.add).then_inc(signal("hg_state"), 1)

            def scores(j, i):
                dve.wait_ge(*seen("hg_scored", 4 * j + i + 1))
                mask = spread(sq(("hg_causal", "hg_32", "hg_64", "hg_128")[i]), TT)
                if i == 0:
                    if j:
                        dve.wait_ge(*seen("hg_o", j))
                    step(dve.tensor_tensor(heads(hg_sum), heads(bank[4][:]), mask, ALU.mult))
                else:
                    t = hg_qe
                    step(dve.tensor_tensor(heads(t), heads(bank[4 + i % 2][:]), mask, ALU.mult))
                    step(dve.tensor_tensor(hg_sum, hg_sum, t, ALU.add))

            for j in range(HH):
                q, k, log_f = W(24 + j), W(8 + j), W(16 + j)
                dve.wait_ge(*seen("hg_logf", j + 1))
                dve.tensor_tensor_scan(hg_b16, keep16, log_f, 0.0, ALU.mult, ALU.add).then_inc(signal("hg_b"), 1)
                for b in range(TT):
                    c = slice(b * P, (b + 1) * P)
                    ins = dve.tensor_tensor_scan(hg_b128[:, c], sq("ones"), log_f[:, c], 0.0, ALU.mult, ALU.add)
                ins.then_inc(signal("hg_b"), 1)
                exps(2)
                dve.tensor_tensor(hg_qe, q, hg_e, ALU.mult)
                dve.tensor_tensor(hg_ke, k, hg_e2, ALU.mult).then_inc(signal("hg_qk"), 1)
                if j:
                    states(j - 1)
                dve.wait_ge(*seen("hg_b", 2 * j + 2))
                for i, span in enumerate(SPANS):
                    dve.wait_ge(*seen("hg_qk", 4 * j + i + 1))
                    bs = hg_b128.rearrange("p (a n) -> p a n", n=span)
                    dve.tensor_tensor(hg_e.rearrange("p (a n) -> p a n", n=span), bs,
                                      spread(bs[:, :, span // 2 - 1], span, at=2), ALU.subtract)\
                        .then_inc(signal("hg_d"), 1)
                    scores(j, i)
                    exps(1)
                    dve.wait_ge(*seen("hg_d", 4 * j + i + 1))
                    dve.tensor_tensor(hg_qe, q, hg_e, ALU.mult)
                    dve.tensor_tensor(hg_ke, k, hg_e, ALU.mult).then_inc(signal("hg_qk"), 1)
                dve.wait_ge(*seen("hg_qk", 4 * j + 4))
                bs = hg_b128.rearrange("p (a n) -> p a n", n=P)
                dve.tensor_tensor(hg_e.rearrange("p (a n) -> p a n", n=P), spread(bs[:, :, P - 1], P, at=2), bs,
                                  ALU.subtract).then_inc(signal("hg_d"), 1)
                scores(j, 3)
                exps(3)
                dve.tensor_tensor(q, q, hg_e2, ALU.mult)
                dve.tensor_tensor(k, k, hg_e, ALU.mult).then_inc(signal("hg_kend"), 1)
            states(HH - 1)
            for j in range(HH):
                r = W(43 + 3 * (j % 2))
                dve.wait_ge(*seen("hg_std", j + 1))
                step(dve.reciprocal(r, r))
                step(dve.scalar_tensor_tensor(W(24 + j), W(24 + j), col("hg_norm_g_2", j), r, ALU.mult, ALU.mult))
                dve.tensor_tensor(W(24 + j), W(24 + j), h[:, j, :], ALU.mult).then_inc(signal("y_b"), 1)
            for j, tile in enumerate(tiles_of(*L["wb2"])):
                b = read_tile(dve, tile, j == 0)
                dve.tensor_tensor(W(16 + j), W(16 + j), b[:], ALU.mult).then_inc(sem("tile_read"), 1)
                dve.wait_ge(sem("tile_read"), tile + 1)
                dve.tensor_tensor(W(j), W(j), W(16 + j), ALU.add).then_inc(signal("merged"), 1)
            for j, tile in enumerate(tiles_of(*L["wo2"])):
                b = read_tile(dve, tile)
                dve.scalar_tensor_tensor(X(j), X(j), ALPHA, b[:], ALU.mult, ALU.add).then_inc(sem("tile_read"), 1)

        def hg_act(act):
            step = ordered(act, "hg_act")
            tiles = tiles_of(*L["g2"])

            def copies(j, what):
                if what == "k":
                    act.wait_ge(*seen("hg_turned", j + 1))
                    act.activation(W(16 + j), bank[6][:], ACT.Copy).then_inc(signal("hg_ktok"), 1)
                else:
                    act.wait_ge(*seen("hg_o", j + 1))
                    act.activation(W(24 + j), bank[5][:], ACT.Copy).then_inc(signal("hg_out"), 1)

            for j in range(HH):
                if j:
                    copies(j - 1, "k")
                act.wait_ge(*seen("hg_b", 2 * j + 1))
                act.activation(hg_e, hg_b16, ACT.Exp).then_inc(signal("hg_exp"), 1)
                act.activation(hg_e2, hg_b16, ACT.Exp, scale=-1.0).then_inc(signal("hg_exp"), 1)
                if j:
                    copies(j - 1, "o")
                for i in range(3):
                    act.wait_ge(*seen("hg_d", 4 * j + i + 1))
                    step(act.activation(hg_e, hg_e, ACT.Abs))
                    act.activation(hg_e, hg_e, ACT.Exp, scale=-1.0).then_inc(signal("hg_exp"), 1)
                act.activation(hg_e2, hg_b128, ACT.Exp).then_inc(signal("hg_exp"), 1)
                act.activation(decays[:, 4 * j:4 * j + 4], hg_b128.rearrange("p (a n) -> p a n", n=P)[:, :, P - 1],
                               ACT.Exp).then_inc(signal("hg_exp"), 1)
                act.wait_ge(*seen("hg_d", 4 * j + 4))
                act.activation(hg_e, hg_e, ACT.Exp).then_inc(signal("hg_exp"), 1)
                b = read_tile(act, tiles[j], j == 0)
                act.activation(h[:, j, :], b[:], ACT.Silu, bias=col("b_in_2", 40 + j)).then_inc(sem("tile_read"), 1)
            copies(HH - 1, "k")
            copies(HH - 1, "o")

            def square(j):
                if j >= 2:
                    act.wait_ge(*seen("hg_summed", j - 1))
                act.activation(W(42 + 2 * (j % 2)), W(24 + j), ACT.Square).then_inc(signal("hg_squared"), 1)

            def std(j):
                act.wait_ge(*seen("hg_summed", j + 1))
                if j >= 2:
                    act.wait_ge(*seen("y_b", j - 1))
                act.activation(W(43 + 3 * (j % 2)), bank[4 + j % 2][:], ACT.Sqrt, bias=eps, scale=1.0 / P)\
                    .then_inc(signal("hg_std"), 1)

            act.wait_ge(*seen("hg_out", HH))
            square(0)
            for j, tile in enumerate(tiles_of(*L["gb2"])):
                b = read_tile(act, tile)
                act.activation(W(16 + j), b[:], ACT.Sigmoid, bias=col("b_in_2", 56 + j)).then_inc(sem("tile_read"), 1)
                if j + 1 < HH:
                    square(j + 1)
                std(j)

        FFN = [i for i in range(0, D_FF2, 512)]
        gate_tiles = [t for i in FFN for t in tiles_of(*L[f"fg{i}"])]
        lam_sum, neg_lam = small[:, 113:115], small[:, 115:116]
        up_tiles = [t for i in FFN for t in tiles_of(*L[f"fu{i}"])]
        p_rows = A[:, 32:34, :].rearrange("p a n -> p (a n)").rearrange("p (t n) -> p t n", t=TT)
        p_t = lambda k: W(34 + k)
        two = lambda i: A[:, i:i + 2, :].rearrange("p a n -> p (a n)")
        pg_slices = tile_slices(*L["pg2"])
        gate_up = [(name, i) for i in FFN for name in ("fg", "fu")]
        gate_up_slices = {(name, i): tile_slices(*L[f"{name}{i}"]) for name, i in gate_up}
        ffn_slices = pg_slices + [s for key in gate_up for s in gate_up_slices[key]]
        for i, s in enumerate(ffn_slices):
            s.before = ffn_slices[i - 2] if i >= 2 else None
        down_slices = deep_slices(*L["down2"])
        DEEP2 = len(down_slices) // 2
        ffn_high = lambda slot: two((30, 46)[slot])
        x_low = lambda k: W(36 + k)
        deep_rhs_high = lambda slot: h[:, 2 * slot:2 * slot + 2, :].rearrange("p a n -> p (a n)")
        deep_rhs_low = lambda slot: h[:, 4 + 2 * slot:6 + 2 * slot, :].rearrange("p a n -> p (a n)")

        def ffn2_pe(pe):
            pe.wait_ge(sem("p_in"), 16)
            for k in range(2):
                for t in range(TT):
                    mm = pe.transpose(bank[6 + k][:, t * P:(t + 1) * P], p_rows[:, t, k * P:(k + 1) * P], sq("ident"))
                mm.then_inc(signal("p_turned"), 1)
            project_split(pe, pg_slices, ffn_high, Hn, x_low, first=lambda k: pe.wait_ge(*seen("x1_split", k + 1)))
            pe.wait_ge(*seen("p_ready", 2))
            project(pe, L["ple2"], p_t)
            for n, i in enumerate(FFN):
                project_split(pe, gate_up_slices["fg", i], ffn_high, Hn, x_low)
                sum_pe(pe, L[f"ada3{2 * n}"][0])
                project_split(pe, gate_up_slices["fu", i], ffn_high, Hn, x_low)
                sum_pe(pe, L[f"ada3{2 * n + 1}"][0])
            project_deep_split(pe, down_slices, ffn_high, deep_rhs_high, deep_rhs_low)

        def ffn2_act(act):
            for k in range(2):
                act.wait_ge(*seen("p_turned", k + 1))
                act.activation(p_t(k), bank[6 + k][:], ACT.Copy).then_inc(signal("p_ready"), 1)
            for s in ffn_slices[:2]:
                split_high(act, s, ffn_high)
            for j, tile in enumerate(tiles_of(*L["pg2"])):
                split_high(act, ffn_slices[j + 2], ffn_high)
                b = read_tile(act, tile, j == 0)
                act.activation(W(22 + j), b[:], ACT.Sigmoid, bias=col("b_ple_gate_2", j)).then_inc(sem("tile_read"), 1)
            at, q = 0, len(pg_slices) + 2
            for n, i in enumerate(FFN):
                for j, tile in enumerate(tiles_of(*L[f"fg{i}"])):
                    split_high(act, ffn_slices[q], ffn_high)
                    q += 1
                    b = read_tile(act, tile, n == j == 0)
                    act.activation(W(at), b[:], ACT.Silu).then_inc(sem("tile_read"), 1)
                    at += 1
                ada_act(act, L[f"ada3{2 * n}"][0])
                for _ in tiles_of(*L[f"fu{i}"]):
                    if q < len(ffn_slices):
                        split_high(act, ffn_slices[q], ffn_high)
                        q += 1
                ada_act(act, L[f"ada3{2 * n + 1}"][0], first=True)
            act.wait_ge(*seen("lam_sums", 1))
            act.activation(lam_sum, lam_sum, ACT.Exp).then_inc(signal("lam_exp"), 1)
            act.wait_ge(sem("tile_read"), up_tiles[-1] + 1)
            for j, s in enumerate(down_slices):
                split_high(act, s, ffn_high, two(2 * (j % DEEP2)), deep_rhs_high)

        def down_out(dve, half):
            for j, tile in list(enumerate(tiles_of(*L["down2"])))[4 * half:4 * half + 4]:
                b = read_tile(dve, tile, j == 0)
                dve.scalar_tensor_tensor(X(j), X(j), ALPHA, b[:], ALU.mult, ALU.add).then_inc(sem("tile_read"), 1)
                dve.wait_ge(sem("tile_read"), tile + 1)
                dve.tensor_tensor(X(j), X(j), W(22 + j), ALU.add).then_inc(signal("x_ffn2"), 1)

        def ffn2_dve(dve):
            step = ordered(dve, "ffn2_dve")
            for s in ffn_slices[:2]:
                split_low(dve, s, ffn_high)
            for k in range(KD):
                dve.wait_ge(*norm_at("ln1", "out", k + 1))
                step(dve.tensor_copy(parts(Hn(k)), X(k)))
                dve.tensor_tensor(parts(x_low(k)), X(k), parts(Hn(k)), ALU.subtract).then_inc(signal("x1_split"), 1)
            for s in ffn_slices[2:len(pg_slices) + 2]:
                split_low(dve, s, ffn_high)
            for j, tile in enumerate(tiles_of(*L["ple2"])):
                b = read_tile(dve, tile, j == 0)
                dve.tensor_tensor(W(22 + j), W(22 + j), b[:], ALU.mult).then_inc(sem("tile_read"), 1)
            at, q = 0, len(pg_slices) + 2
            for i in FFN:
                for _ in tiles_of(*L[f"fg{i}"]):
                    split_low(dve, ffn_slices[q], ffn_high)
                    q += 1
                for j, tile in enumerate(tiles_of(*L[f"fu{i}"])):
                    b = read_tile(dve, tile, j == 0)
                    dve.tensor_tensor(W(at), W(at), b[:], ALU.mult).then_inc(sem("tile_read"), 1)
                    at += 1
                    if q < len(ffn_slices):
                        split_low(dve, ffn_slices[q], ffn_high)
                        q += 1
            ada_dve(dve, L["ada311"][0], 0, 48, col("b_ada_3", 0, 48),
                    ((0, col("pre_norm1_3", 0, 8)), (1, col("pre_norm2_3", 0, 8))), "ada3_ready")
            lam_dve(dve)
            for j, s in enumerate(down_slices):
                split_low(dve, s, ffn_high, two(2 * (j % DEEP2)), deep_rhs_high, deep_rhs_low)
                if j == DEEP2 + 1:
                    down_out(dve, 0)
            down_out(dve, 1)

        def block2_pe(pe):
            norm_pe(pe, "ln0", X, TMP, ready=(norm_at("n3", "scaled", KD),))
            spatial_pe(pe)
            gmlp_pe(pe)
            hg_pe(pe)
            norm_pe(pe, "ln1", X, TMP, ready=((sem("tile_read"), L["wo2"][-1].first_tile + 4),))
            ffn2_pe(pe)
            norm_pe(pe, "ln2", X, TMP, ready=(seen("x_ffn2", KD),))

        def block2_pool(pool):
            sum_pool(pool, [L[f"ada3{i}"][0] for i in range(12)], small[:, 86:94], "cond3")

        def block2_act(act):
            block2_loads(act)
            norm_act(act, "ln0", X, TMP, W(46), ln_eps, shift=lambda k: col("ln0_b_2", k), dst=X)
            lb_act(act)
            gmlp_act(act)
            hg_in_act(act)
            hg_act(act)
            norm_act(act, "ln1", X, TMP, W(46), ln_eps, shift=lambda k: col("ln1_b_2", k), dst=X)
            act.dma_start(p_rows, w["p_2"].rearrange("b (t p) n -> p (b t) n", p=P)).then_inc(sem("p_in"), 16)
            ffn2_act(act)
            norm_act(act, "ln2", X, TMP, W(46), ln_eps, shift=lambda k: col("ln2_b_2", k), dst=X)

        def block2_dve(dve):
            lb_dve(dve)
            norm_dve(dve, "ln0", X, W(46), lambda k: col("ln0_g_2", k), X, xc=X)
            spatial_dve(dve)
            gmlp_dve(dve)
            hg_in_dve(dve)
            hg_dve(dve)
            norm_dve(dve, "ln1", X, W(46), lambda k: col("ln1_g_2", k), X, xc=X)
            ffn2_dve(dve)
            norm_dve(dve, "ln2", X, W(46), lambda k: col("ln2_g_2", k), X, xc=X)

        def block2_sync(sp):
            sp.wait_ge(sem("moe_written"), 1)
            load_weights(sp, order[L["v2"][0].index:])

        glu_gate = (8, 9, 10, 11, 44, 45, 46, 47)
        cos, sin = W(12), W(13)
        gain1, gain2 = small[:, 96:104], small[:, 104:112]
        scaled_head = small[:, 116:117]
        d_max = lambda u: small[:, 128 + 2 * (u % 4):130 + 2 * (u % 4)]
        d_sum = lambda u: small[:, 136 + 2 * (u % 4):138 + 2 * (u % 4)]
        d_rec = lambda u: small[:, 144 + 2 * (u % 4):146 + 2 * (u % 4)]
        d_mix = lambda u: small[:, 152 + u % 4:153 + u % 4]
        d_square = small[:, 160:168]
        probs = lambda u, i: h[:, 2 * (u % 2) + i, :]
        probs_t = lambda u: h[:, 4 + u % 2, :]
        att_rows = h[:, 6:8, :].rearrange("p a n -> p (a n)")
        v3_tok = lambda t: A[:, 40 + 2 * t:42 + 2 * t, :].rearrange("p a n -> p (a n)")
        SCALE3 = 64 ** -0.5
        dunits = [(q, i) for q in range(TT) for i in range(DIFF_H)]
        rope_tiles = tiles_of(*L["q3"], *L["k3"])

        def lam_dve(dve):
            step = ordered(dve, "lam_dve")
            for i in range(2):
                t = W(44)[:, 0:64]
                step(dve.tensor_tensor(t, row(f"lambda_q{i + 1}_3", 64), row(f"lambda_k{i + 1}_3", 64), ALU.mult))
                ins = dve.tensor_reduce(lam_sum[:, i:i + 1], t, AX_X, ALU.add)
                if i == 0:
                    step(ins)
            ins.then_inc(signal("lam_sums"), 1)
            dve.wait_ge(*seen("lam_exp", 1))
            step(dve.tensor_tensor(neg_lam, lam_sum[:, 1:2], lam_sum[:, 0:1], ALU.subtract))
            step(dve.tensor_scalar(neg_lam, neg_lam, -LAM_INIT, None, ALU.add))
            step(dve.tensor_scalar(scaled_head, col("head_norm_3"), 1.0 - LAM_INIT, None, ALU.mult))
            step(dve.tensor_tensor(gain1, mod[:, 16:24], col("post_norm1_3", 0, 8), ALU.mult))
            step(dve.tensor_tensor(gain2, mod[:, 40:48], col("post_norm2_3", 0, 8), ALU.mult))

        glu_slices = tile_slices(*(L[f"{n}3{i}"][0] for i in range(2) for n in ("ub", "ua")))
        q_slices = tile_slices(*L["q3"])
        in3_slices = glu_slices + q_slices
        for i, s in enumerate(in3_slices):
            s.before = in3_slices[i - 2] if i >= 2 else None
        in3_high = lambda slot: two(40 + 2 * slot)
        in3_x_high = lambda k: W(32 + k)

        def block3_pool(pool):
            for s in in3_slices:
                split_low(pool, s, in3_high)
            pool.wait_ge(sem("tile_ready"), L["q3"][-1].first_tile + 4)
            for k in range(KD):
                pool.tensor_tensor(Hn(k), parts(in3_x_high(k)), parts(Hn(k)), ALU.add).then_inc(sem("h3_whole"), 1)

        def in3_pe(pe):
            project_split(pe, glu_slices, in3_high, in3_x_high, Hn,
                          first=lambda k: pe.wait_ge(*seen("h3_in_split", k + 1)))

            def rotate(n):
                pe.wait_ge(sem("tile_read"), rope_tiles[n] + 1)
                if n == 0:
                    pe.wait_ge(sem("tables_in"), 32)
                if n >= 2:
                    pe.wait_ge(*seen("roped", n - 1))
                pe.matmul(bank[4 + n % 2][:], sq("rope_rot"), W(14 + n % 2), start=True, stop=True)\
                    .then_inc(signal("rope_rotated"), 1)

            def whole(k):
                pe.wait_ge(sem("h3_whole"), k + 1)
                return Hn(k)

            n = 0
            for s in q_slices:
                project_split(pe, [s], in3_high, in3_x_high, Hn,
                              between=(lambda n=n: rotate(n - 1)) if n else None)
                n += 1
            for g in L["k3"]:
                for m in range(4):
                    in_pairs(pe, g, m, whole if n == 8 else Hn, lambda i, n=n: rotate(n - 1) if i == 0 else None)
                    n += 1
            rotate(n - 1)
            for g in L["v3"]:
                weights_here(pe, g)
                project_tokens(pe, g, lambda k, t: Hn(k)[:, t * P:(t + 1) * P], 0, 512, g.first_tile)
            project(pe, L["cg3"], Hn)
            norm_pe(pe, "conv_ln", lambda k: W(16 + k), lambda i: W(10 + i), ready=(seen("u_conved", KD),))
            project(pe, L["ag3"], Hn)

        def in3_act(act):
            for s in in3_slices[:2]:
                split_high(act, s, in3_high)
            for i in range(2):
                if i:
                    for s in in3_slices[6:10]:
                        split_high(act, s, in3_high)
                for m, tile in enumerate(tiles_of(*L[f"ub3{i}"])):
                    split_high(act, in3_slices[8 * i + m + 2], in3_high)
                    b = read_tile(act, tile, m == 0)
                    act.activation(W(glu_gate[4 * i + m]), b[:], ACT.Sigmoid).then_inc(sem("tile_read"), 1)
            for s in in3_slices[14:18]:
                split_high(act, s, in3_high)
            act.dma_start(cos, w["tables"][0]).then_inc(sem("tables_in"), 16)
            act.dma_start(sin, w["tables"][1]).then_inc(sem("tables_in"), 16)
            for n, tile in enumerate(rope_tiles):
                if 18 + n < len(in3_slices):
                    split_high(act, in3_slices[18 + n], in3_high)
                b = read_tile(act, tile, n == 0)
                if n >= 2:
                    act.wait_ge(*seen("roped", n - 1))
                act.activation(W(14 + n % 2), b[:], ACT.Copy).then_inc(sem("tile_read"), 1)
            for j, g in enumerate(L["v3"]):
                for t in range(TT):
                    b = read_tile(act, g.first_tile + t)
                    act.activation(v3_tok(t)[:, 512 * j:512 * j + 512], b[:], ACT.Copy).then_inc(sem("tile_read"), 1)
            act.wait_ge(*seen("u_conved", KD))
            for j, tile in enumerate(tiles_of(*L["cg3"])):
                b = read_tile(act, tile)
                act.activation(W(j), b[:], ACT.Sigmoid).then_inc(sem("tile_read"), 1)
            act.wait_ge(*seen("roped", 2 * KD))
            norm_act(act, "conv_ln", lambda k: W(16 + k), lambda i: W(10 + i), W(12), eps,
                     shift=lambda k: col("conv_ln_b_3", k), dst=lambda k: W(16 + k), func=ACT.Silu)
            for j, tile in enumerate(tiles_of(*L["ag3"])):
                b = read_tile(act, tile)
                act.activation(W(8 + j), b[:], ACT.Sigmoid).then_inc(sem("tile_read"), 1)

        def in3_dve(dve):
            step = ordered(dve, "in3_dve")

            def conv(c, first, last):
                u, y = W(c), W(16 + c)
                for i in range(first, last):
                    tap = col("conv_w_3", 8 * (CONV3 - 1 - i) + c)
                    if i == 0:
                        ins = dve.tensor_scalar(y, u, tap, col("conv_b_3", c), ALU.mult, ALU.add)
                    else:
                        ins = dve.scalar_tensor_tensor(y[:, i:T], u[:, 0:T - i], tap, y[:, i:T], ALU.mult, ALU.add)
                    if i < CONV3 - 1:
                        step(ins)
                    else:
                        ins.then_inc(signal("u_conved"), 1)

            def glu(i):
                for m, tile in enumerate(tiles_of(*L[f"ua3{i}"])):
                    b = read_tile(dve, tile, m == 0)
                    c = 4 * i + m
                    dve.tensor_tensor(W(c), b[:], W(glu_gate[c]), ALU.mult).then_inc(sem("tile_read"), 1)
                dve.wait_ge(sem("tile_read"), tile + 1)

            for k in range(KD):
                dve.wait_ge(*norm_at("pre1", "out", k + 1))
                step(dve.tensor_copy(parts(in3_x_high(k)), Hn(k)))
                dve.tensor_tensor(parts(Hn(k)), Hn(k), parts(in3_x_high(k)), ALU.subtract)\
                    .then_inc(signal("h3_in_split"), 1)
            glu(0)
            conv(0, 0, CONV3)
            conv(1, 0, CONV3)
            glu(1)
            pieces = [(c, a, min(a + 8, CONV3)) for c in range(2, KD) for a in range(0, CONV3, 8)]
            for n, tile in enumerate(rope_tiles):
                if n and pieces:
                    conv(*pieces.pop(0))
                raw, dst, t = W(14 + n % 2), W(24 + n), W(10 + n % 2)
                dve.wait_ge(sem("tile_read"), tile + 1)
                dve.wait_ge(sem("tables_in"), 32)
                step(dve.tensor_tensor(dst, raw, cos, ALU.mult))
                dve.wait_ge(*seen("rope_rotated", n + 1))
                step(dve.tensor_tensor(t, bank[4 + n % 2][:], sin, ALU.mult))
                dve.tensor_tensor(dst, dst, t, ALU.add).then_inc(signal("roped"), 1)
            for p in pieces:
                conv(*p)
            dve.wait_ge(*seen("u_conved", KD))
            norm_dve(dve, "conv_ln", lambda k: W(16 + k), W(12), lambda k: col("conv_ln_g_3", k),
                     lambda k: W(16 + k), xc=lambda k: W(16 + k))

        def diff_pe(pe):
            pe.wait_ge(sem("tile_read"), L["ag3"][-1].first_tile + 4)
            pe.wait_ge(*norm_at("conv_ln", "scaled", KD))

            def scores(u):
                q, i = dunits[u]
                r, n = 64 * (i % 2), P * (q + 1)
                if u >= 2:
                    pe.wait_ge(*seen("diff_exp", 2 * (u - 1)))
                for j in range(2):
                    mm = pe.matmul(bank[4 + 2 * (u % 2) + j][:, 0:n], W(24 + 4 * j + i // 2)[r:r + 64, q * P:q * P + P],
                                   W(32 + 4 * j + i // 2)[r:r + 64, 0:n], start=True, stop=True)
                mm.then_inc(signal("diff_scores"), 1)

            def turn(u):
                q, i = dunits[u]
                pe.wait_ge(*seen("diff_probs", u + 1))
                if u >= 2:
                    pe.wait_ge(*seen("diff_probs_t", u - 1))
                for k in range(q + 1):
                    mm = pe.transpose(head(bank[u % 2][:], k), head(probs(u, 0), k), sq("ident"))
                mm.then_inc(signal("diff_turned"), 1)

            def mix(u):
                q, i = dunits[u]
                pe.wait_ge(*seen("diff_probs_t", u + 1))
                if u >= 2:
                    pe.wait_ge(*seen("diff_squared", u - 1))
                if u % DIFF_H < 2 and q:
                    pe.wait_ge(*seen("att", 8 * q))
                for k in range(q + 1):
                    mm = pe.matmul(bank[2 + u % 2][:, 0:P], head(probs_t(u), k), v3_tok(k)[:, i * P:(i + 1) * P],
                                   start=(k == 0), stop=(k == q))
                mm.then_inc(signal("diff_mixed"), 1)

            def back(q):
                pe.wait_ge(*seen("diff_rows", q + 1))
                for i in range(2):
                    for k in range(4):
                        mm = pe.transpose(head(bank[2 + i][:], k), att_rows[:, (4 * i + k) * P:(4 * i + k + 1) * P],
                                          sq("ident"))
                    mm.then_inc(signal("diff_back"), 1)

            scores(0)
            scores(1)
            for u in range(len(dunits)):
                if u + 2 < len(dunits):
                    scores(u + 2)
                turn(u)
                if u:
                    mix(u - 1)
                if u and u % DIFF_H == 0:
                    back(u // DIFF_H - 1)
            mix(len(dunits) - 1)
            back(TT - 1)

        def diff_act(act):
            def exps(u):
                q, i = dunits[u]
                n = P * (q + 1)
                act.wait_ge(*seen("diff_max", u + 1))
                if u >= 2:
                    act.wait_ge(*seen("diff_turned", u - 1))
                for j in range(2):
                    act.activation(probs(u, j)[:, 0:n], bank[4 + 2 * (u % 2) + j][:, 0:n], ACT.Exp,
                                   bias=d_max(u)[:, j:j + 1], scale=SCALE3, accum_out=d_sum(u)[:, j:j + 1])\
                        .then_inc(signal("diff_exp"), 1)

            def copy_t(u):
                n = P * (dunits[u][0] + 1)
                act.wait_ge(*seen("diff_turned", u + 1))
                if u >= 2:
                    act.wait_ge(*seen("diff_mixed", u - 1))
                act.activation(probs_t(u)[:, 0:n], bank[u % 2][:, 0:n], ACT.Copy).then_inc(signal("diff_probs_t"), 1)

            def rows_of(u):
                q, i = dunits[u]
                act.wait_ge(*seen("diff_mixed", u + 1))
                if i == 0 and q:
                    act.wait_ge(*seen("diff_back", 2 * q))
                r = d_rec(u)[:, 0:1]
                o = bank[2 + u % 2][:, 0:P]
                act.activation(att_rows[:, i * P:(i + 1) * P], o, ACT.Copy, scale=r)
                act.activation(bank[2 + u % 2][:, P:2 * P], o, ACT.Square, scale=r, accum_out=d_square[:, i:i + 1])\
                    .then_inc(signal("diff_squared"), 1)
                if i == DIFF_H - 1:
                    act.wait_ge(*seen("diff_squared", u + 1))
                    act.activation(d_square, d_square, ACT.Sqrt, bias=eps, scale=1.0 / P)\
                        .then_inc(signal("diff_std"), 1)

            for u in range(len(dunits)):
                exps(u)
                if u:
                    copy_t(u - 1)
                if u >= 2:
                    rows_of(u - 2)
            u = len(dunits)
            copy_t(u - 1)
            rows_of(u - 2)
            rows_of(u - 1)

        def diff_dve(dve):
            step = ordered(dve, "diff_dve")

            def maxes(u):
                q, i = dunits[u]
                n = P * (q + 1)
                dve.wait_ge(*seen("diff_scores", u + 1))
                for j in range(2):
                    d = bank[4 + 2 * (u % 2) + j][:, n - P:n]
                    ins = dve.tensor_tensor(d, d, sq("causal_add"), ALU.add)
                step(ins)
                for j in range(2):
                    ins = dve.tensor_reduce(d_max(u)[:, j:j + 1], bank[4 + 2 * (u % 2) + j][:, 0:n], AX_X, ALU.max,
                                            negate=True)
                step(ins)
                dve.tensor_scalar(d_max(u), d_max(u), SCALE3, None, ALU.mult).then_inc(signal("diff_max"), 1)

            def combine(u):
                n = P * (dunits[u][0] + 1)
                dve.wait_ge(*seen("diff_exp", 2 * (u + 1)))
                step(dve.reciprocal(d_rec(u), d_sum(u)))
                step(dve.scalar_tensor_tensor(d_mix(u), d_sum(u)[:, 0:1], neg_lam, d_rec(u)[:, 1:2], ALU.mult,
                                              ALU.mult))
                dve.scalar_tensor_tensor(probs(u, 0)[:, 0:n], probs(u, 1)[:, 0:n], d_mix(u), probs(u, 0)[:, 0:n],
                                         ALU.mult, ALU.add).then_inc(signal("diff_probs"), 1)

            def norm_rows(q):
                dve.wait_ge(*seen("diff_std", q + 1))
                step(dve.reciprocal(d_square, d_square))
                rows8 = att_rows.rearrange("p (i n) -> p i n", n=P)
                dve.tensor_tensor(rows8, rows8, spread(d_square, P, at=2), ALU.mult).then_inc(signal("diff_rows"), 1)

            def to_gates(q):
                c = slice(q * P, (q + 1) * P)
                for k in range(KD):
                    if k % 4 == 0:
                        dve.wait_ge(*seen("diff_back", 2 * q + k // 4 + 1))
                    dve.scalar_tensor_tensor(W(8 + k)[:, c], head(bank[2 + k // 4][:], k % 4), scaled_head,
                                             W(8 + k)[:, c], ALU.mult, ALU.mult).then_inc(signal("att"), 1)

            for u in range(len(dunits)):
                maxes(u)
                if u:
                    combine(u - 1)
                if u % DIFF_H == 1 and u > 1:
                    norm_rows(u // DIFF_H - 1)
                    to_gates(u // DIFF_H - 1)
            combine(len(dunits) - 1)
            norm_rows(TT - 1)
            to_gates(TT - 1)

        ff1_slices = tile_slices(*L["ff1"])
        ff2_slices = deep_slices(*L["ff2"])
        DEEP3 = len(ff2_slices) // 2
        ff1_high = lambda slot: two(40 + 2 * slot)
        ff2_rhs = lambda j: two(2 * (j % DEEP3))

        def out3_pe(pe):
            pe.wait_ge(*norm_at("conv_ln", "out", KD))
            pe.wait_ge(*seen("att", 8 * TT))
            project(pe, L["co3"], lambda k: W(16 + k))
            pe.wait_ge(*seen("merged3", KD))
            project(pe, L["wo3"], W)
            norm_pe(pe, "post1", None, TMP)
            norm_pe(pe, "pre2", None, TMP)
            project_split(pe, ff1_slices, ff1_high, lambda k: W(32 + k), Hn,
                          first=lambda k: pe.wait_ge(*seen("h3_split", k + 1)))
            project_deep_split(pe, ff2_slices, ff1_high, deep_rhs_high, deep_rhs_low)
            norm_pe(pe, "post2", None, TMP)

        def ff2_out(act, half):
            for j, tile in enumerate(tiles_of(*L["ff2"])[4 * half:4 * half + 4]):
                b = read_tile(act, tile, half == j == 0)
                act.activation(W(32 + 4 * half + j), b[:], ACT.Copy).then_inc(sem("tile_read"), 1)

        def out3_act(act):
            for j, tile in enumerate(tiles_of(*L["wo3"])):
                b = read_tile(act, tile, j == 0)
                act.activation(W(16 + j), b[:], ACT.Copy).then_inc(sem("tile_read"), 1)
            norm_act(act, "post1", lambda k: W(16 + k), TMP, W(46), eps,
                     ready=((sem("tile_read"), L["wo3"][-1].first_tile + 4),))
            act.wait_ge(*norm_at("post1", "scaled", KD))
            norm_act(act, "pre2", X, TMP, W(46), eps, shift=lambda k: mod[:, 24 + k:25 + k], dst=Hn,
                     ready=(seen("x_att", KD),))
            for s in ff1_slices[:2]:
                split_high(act, s, ff1_high)
            for j, tile in enumerate(tiles_of(*L["ff1"])):
                if j + 2 < len(ff1_slices):
                    split_high(act, ff1_slices[j + 2], ff1_high)
                act.wait_ge(sem("tile_read"), tile + 1)
                act.activation(W(j), W(j), ACT.Square).then_inc(signal("ff1_squared"), 1)
            act.wait_ge(*seen("ff1_squared", D_FF3 // P))
            for j, s in enumerate(ff2_slices):
                if j < 2:
                    act.wait_ge(sem("tile_ready"), L["ff1"][-1].first_tile + 3 + j)
                split_high(act, s, ff1_high, ff2_rhs(j), deep_rhs_high)
                if j == DEEP3 + 1:
                    ff2_out(act, 0)
            ff2_out(act, 1)
            norm_act(act, "post2", lambda k: W(32 + k), TMP, W(46), eps,
                     ready=((sem("tile_read"), L["ff2"][-1].first_tile + 4),))

        def out3_dve(dve):
            step = ordered(dve, "out3_dve")
            for j, tile in enumerate(tiles_of(*L["co3"])):
                b = read_tile(dve, tile, j == 0)
                dve.scalar_tensor_tensor(W(j), b[:], col("conv_b_out_3", j), W(j), ALU.add, ALU.mult)\
                    .then_inc(sem("tile_read"), 1)
                dve.wait_ge(sem("tile_read"), tile + 1)
                dve.tensor_tensor(W(j), W(j), W(8 + j), ALU.add).then_inc(signal("merged3"), 1)
            norm_dve(dve, "post1", lambda k: W(16 + k), W(46), lambda k: gain1[:, k:k + 1], lambda k: W(16 + k))
            for k in range(KD):
                dve.wait_ge(*norm_at("post1", "scaled", k + 1))
                dve.tensor_tensor(X(k), X(k), W(16 + k), ALU.add).then_inc(signal("x_att"), 1)
            norm_dve(dve, "pre2", X, W(46), lambda k: mod[:, 32 + k:33 + k], Hn)
            for s in ff1_slices[:2]:
                split_low(dve, s, ff1_high)
            for k in range(KD):
                dve.wait_ge(*norm_at("pre2", "out", k + 1))
                step(dve.tensor_copy(parts(W(32 + k)), Hn(k)))
                dve.tensor_tensor(parts(Hn(k)), Hn(k), parts(W(32 + k)), ALU.subtract).then_inc(signal("h3_split"), 1)
            for j, tile in enumerate(tiles_of(*L["ff1"])):
                b = read_tile(dve, tile, j == 0)
                dve.tensor_scalar(W(j), b[:], 0.0, None, ALU.max).then_inc(sem("tile_read"), 1)
                if j + 2 < len(ff1_slices):
                    split_low(dve, ff1_slices[j + 2], ff1_high)
            for j, s in enumerate(ff2_slices):
                split_low(dve, s, ff1_high, ff2_rhs(j), deep_rhs_high, deep_rhs_low)
            norm_dve(dve, "post2", lambda k: W(32 + k), W(46), lambda k: gain2[:, k:k + 1], lambda k: W(32 + k))
            for k in range(KD):
                dve.wait_ge(*norm_at("post2", "scaled", k + 1))
                dve.tensor_tensor(X(k), X(k), W(32 + k), ALU.add).then_inc(signal("x_done"), 1)

        def block3_pe(pe):
            norm_pe(pe, "pre1", X, TMP)
            in3_pe(pe)
            diff_pe(pe)
            out3_pe(pe)

        def block3_act(act):
            norm_act(act, "pre1", X, TMP, W(46), eps, shift=lambda k: mod[:, k:k + 1], dst=Hn,
                     ready=(norm_at("ln2", "out", KD),))
            in3_act(act)
            diff_act(act)
            out3_act(act)

        def block3_dve(dve):
            norm_dve(dve, "pre1", X, W(46), lambda k: mod[:, 8 + k:9 + k], Hn, ready=(norm_at("ln2", "out", KD),))
            in3_dve(dve)
            diff_dve(dve)
            out3_dve(dve)

        def final_pe(pe):
            pe.wait_ge(*final_ready)
            for i in range(2 * TT):
                if i >= 2:
                    pe.wait_ge(sem("final_copied"), i - 1)
                for k in range(4):
                    mm = pe.transpose(bank[6 + i % 2][:, k * P:(k + 1) * P],
                                      X(4 * (i % 2) + k)[:, (i // 2) * P:(i // 2 + 1) * P], sq("ident"))
                mm.then_inc(sem("final_turned"), 1)

        def final_act(act):
            for i in range(2 * TT):
                act.wait_ge(sem("final_turned"), i + 1)
                act.activation(W(i), bank[6 + i % 2][:], ACT.Copy).then_inc(sem("final_copied"), 1)

        def final_sync(sp):
            for t in range(TT):
                sp.wait_ge(sem("final_copied"), 2 * t + 2)
                sp.dma_start(out.rearrange("b (t p) n -> t p (b n)", p=P)[t],
                             A[:, 2 * t:2 * t + 2, :].rearrange("p a n -> p (a n)")).then_inc(sem("stored"), 16)
            sp.wait_ge(sem("stored"), 16 * TT)

        sync_program = (block1_sync, block2_sync, final_sync)
        tensor_program = (block1_pe, block2_pe, block3_pe, final_pe)
        scalar_program = (block1_act, block2_act, block3_act, final_act)
        vector_program = (block1_dve, block2_dve, block3_dve)
        pool_program = (block1_pool, block2_pool, block3_pool)
        final_ready = seen("x_done", KD)

        block = ctx.enter_context(nc.Block())

        @block.sync
        def _(sp):
            for f in sync_program:
                f(sp)

        @block.tensor
        def _(pe):
            for f in tensor_program:
                f(pe)

        @block.scalar
        def _(act):
            for f in scalar_program:
                f(act)

        @block.vector
        def _(dve):
            for f in vector_program:
                f(dve)

        @block.gpsimd
        def _(pool):
            for f in pool_program:
                f(pool)


def squares():
    import numpy as np

    s, c = np.arange(P)[:, None], np.arange(P)[None, :]
    chunk = s // GC == c // GC
    hg = s // HC == c // HC
    rot = np.zeros((P, P), np.float32)
    for blk in range(P // 64):
        for j in range(32):
            rot[64 * blk + 32 + j, 64 * blk + j] = -1.0
            rot[64 * blk + j, 64 * blk + 32 + j] = 1.0
    m = {
        "ident": s == c, "ones": s >= 0 * c, "mean": (s >= 0 * c) / D,
        "inc_f": chunk & (c >= s), "inc_b": chunk & (c <= s), "str_f": chunk & (c > s), "str_b": chunk & (c < s),
        "near": s // 16 == c // 16, "far": s // 16 != c // 16, "before": c > s, "hg_causal": hg & (c >= s),
        "rope_rot": rot, "causal_add": np.where(c > s, -BIG, 0.0), "half_lo": (s < 64) & (c >= 0),
        "half_hi": (s >= 64) & (c >= 0), "iota": c + 0 * s, "part": s + 0 * c,
    }
    for n in (32, 64, 128):
        m[f"hg_{n}"] = (s // n == c // n) & (s % n < n // 2) & (c % n >= n // 2)
    return np.stack([np.asarray(m[n], np.float32) for n in SQUARES])


def window_mask():
    import numpy as np

    c, k = np.arange(GRID)[:, None], np.arange(GRID)[None, :]
    first = np.clip(c - 8, 0, GRID - 16)
    return np.where((k >= first) & (k < first + 16), 0.0, -BIG).astype(np.float32)


def rope_tables():
    import numpy as np

    f = np.arange(0, 64, 2, dtype=np.float32)
    inv = (np.float32(10000.0) ** (-f / np.float32(64))).astype(np.float32)
    ang = (np.arange(T, dtype=np.float32)[None, :] * np.tile(inv, 4)[:, None]).astype(np.float32)
    keep = np.broadcast_to((np.arange(T) % HC != 0).astype(np.float32), (P, T))
    return np.stack([np.cos(ang.astype(np.float64)), np.sin(ang.astype(np.float64)), keep]).astype(np.float32)


_DIRECT = ("x", "w_ada", "w_in", "na_rpb", "w_out", "router_group_w", "router_expert_w", "expert_w1", "expert_w3",
           "expert_w2", "p_2", "w_in_2", "gm_w_s_2", "w_a_2", "w_b_2", "w_o_2", "w_ffn_gate_2", "w_ffn_up_2",
           "w_ffn_down_2", "w_ple_2", "w_ple_gate_2", "w_ada_3", "w_in_3", "conv_w_out_3", "w_o_3", "w_ff1_3",
           "w_ff2_3")
_LAYERED = {"x", "p_2"}


def lay_out(inputs):
    import numpy as np

    arrays = {}
    for name in _DIRECT:
        a = np.asarray(inputs[name])
        arrays[name] = np.ascontiguousarray(a if name == "x" else a[0])
    arrays["vectors"] = np.concatenate([np.asarray(inputs[n]).reshape(-1, P) for n, _ in VECTORS])
    arrays["rows"] = np.concatenate([np.asarray(inputs[n]).reshape(-1) for n, _ in ROWS])
    arrays["rows2"] = np.concatenate([np.asarray(inputs[n]).reshape(-1) for n, _ in ROWS2])
    arrays["squares"] = squares()
    arrays["window"] = window_mask()
    arrays["tables"] = rope_tables()
    return arrays


def kernel(**inputs):
    import concourse.bacc as bacc
    from concourse.bass_utils import run_bass_kernel_spmd

    nc = bacc.Bacc("TRN2", target_bir_lowering=False, num_devices=1)
    arrays = lay_out(inputs)
    w = {n: nc.dram_tensor(f"in_{n}", a.shape, mybir.dt.from_np(a.dtype), kind="ExternalInput").ap()
         for n, a in arrays.items()}
    out = nc.dram_tensor("out_x", (1, T, D), F32, kind="ExternalOutput").ap()
    build(nc, w, out)
    r = run_bass_kernel_spmd(nc, [{f"in_{n}": a for n, a in arrays.items()}], core_ids=[0])
    return r.results[0]["out_x"]
```
